# Optimizing a Trainium2 kernel written in Bass

```python
import math
import jax
import jax.numpy as jnp
from jax import lax
import numpy as np

D_MODEL = 1024
BATCH = 1
SEQ = 512
DEPTH = 1
DEC_BATCH = 8
DEC_SEQ = 4
PAST_LEN = 256
PAGE_SIZE = 128

HEAD_DIM = 64
N_HEADS_FOX = 8
N_HEADS_DIL = 8
W_FOX = N_HEADS_FOX * HEAD_DIM
W_DIL = N_HEADS_DIL * HEAD_DIM
D_MIX = W_FOX + W_DIL
N_IN = 3 * W_FOX + 3 * W_DIL + N_HEADS_FOX
DIL_CONFIGS = ((128, 1), (512, 4), (2048, 16))
MAX_WINDOW = 2048
Q_BLOCK = 128
N_BUCKETS = 32
MAX_DISTANCE = 2048
N_KEYS = 128
N_EXPERTS = N_KEYS * N_KEYS
PEER_HEADS = 8
PEER_TOPK = 16
D_QUERY = 256
PEER_BLOCK = 256
RMS_EPS = 1e-6
FORGET_BIAS_INIT = 3.0

kernel_name = "hymba_fox_dilated_peer_step"

def rmsnorm(x, g):
    x32 = x.astype(jnp.float32)
    y = x32 * lax.rsqrt(jnp.mean(x32 * x32, axis=-1, keepdims=True) + RMS_EPS)
    return (y * g.astype(jnp.float32)).astype(x.dtype)

def t5_bucket(dist):
    exact = N_BUCKETS // 2
    d32 = jnp.maximum(dist, 1).astype(jnp.float32)
    large = exact + (jnp.log(d32 / exact) / math.log(MAX_DISTANCE / exact) * (N_BUCKETS - exact)).astype(jnp.int32)
    return jnp.where(dist < exact, dist, jnp.minimum(large, N_BUCKETS - 1))

def dilation_bias(rel_bias, window, dil):
    span = window // dil
    dist = jnp.arange(span + 1, dtype=jnp.int32) * dil
    return rel_bias[t5_bucket(dist)].astype(jnp.float32)

def split_projection(xn, w_in, b_f):
    z = xn @ w_in
    lead = z.shape[:-1]
    cuts = [W_FOX, 2 * W_FOX, 3 * W_FOX, 3 * W_FOX + W_DIL, 3 * W_FOX + 2 * W_DIL, 3 * W_FOX + 3 * W_DIL]
    qa, ka, va, qb, kb, vb, fz = jnp.split(z, cuts, axis=-1)
    fox = lambda t: t.reshape(*lead, N_HEADS_FOX, HEAD_DIM)
    dil = lambda t: t.reshape(*lead, N_HEADS_DIL, HEAD_DIM)
    logf = jax.nn.log_sigmoid(fz.astype(jnp.float32) + b_f.astype(jnp.float32))
    return fox(qa), fox(ka), fox(va), dil(qb), dil(kb), dil(vb), logf

def fox_prompt(q, k, v, logf):
    b, s, h, dh = q.shape
    nb = s // Q_BLOCK
    scale = dh ** -0.5
    k32 = k.astype(jnp.float32)
    v32 = v.astype(jnp.float32)
    cum_t = jnp.cumsum(logf, axis=1).transpose(0, 2, 1)
    q_blocks = q.reshape(b, nb, Q_BLOCK, h, dh).transpose(1, 0, 2, 3, 4)
    c_blocks = cum_t.reshape(b, h, nb, Q_BLOCK).transpose(2, 0, 1, 3)
    k_pos = jnp.arange(s)

    def block(args):
        qi, ci, bi = args
        sc = jnp.einsum("bqhd,bkhd->bhqk", qi.astype(jnp.float32), k32) * scale
        sc = sc + ci[..., :, None] - cum_t[:, :, None, :]
        q_pos = bi * Q_BLOCK + jnp.arange(Q_BLOCK)
        sc = jnp.where(k_pos[None, :] <= q_pos[:, None], sc, -jnp.inf)
        p = jax.nn.softmax(sc, axis=-1)
        return jnp.einsum("bhqk,bkhd->bqhd", p, v32)

    o = lax.map(block, (q_blocks, c_blocks, jnp.arange(nb)))
    return o.transpose(1, 0, 2, 3, 4).reshape(b, s, h, dh)

def fox_sample(q, k_new, v_new, logf_new, k_past, v_past, logf_past):
    past = k_past.shape[1]
    n_new = q.shape[1]
    scale = q.shape[-1] ** -0.5
    q32 = q.astype(jnp.float32)
    cum = jnp.cumsum(jnp.concatenate([logf_past.astype(jnp.float32), logf_new], axis=1), axis=1).transpose(0, 2, 1)
    sc = jnp.concatenate([
        jnp.einsum("bqhd,bkhd->bhqk", q32, k_past.astype(jnp.float32)),
        jnp.einsum("bqhd,bkhd->bhqk", q32, k_new.astype(jnp.float32))], axis=-1) * scale
    sc = sc + cum[:, :, past:, None] - cum[:, :, None, :]
    q_pos = past + jnp.arange(n_new)
    k_pos = jnp.arange(past + n_new)
    sc = jnp.where(k_pos[None, :] <= q_pos[:, None], sc, -jnp.inf)
    p = jax.nn.softmax(sc, axis=-1)
    return (jnp.einsum("bhqk,bkhd->bqhd", p[..., :past], v_past.astype(jnp.float32))
            + jnp.einsum("bhqk,bkhd->bqhd", p[..., past:], v_new.astype(jnp.float32)))

def dilated_prompt_branch(q, k, v, bias, window, dil):
    b, s, h, dh = q.shape
    span = window // dil
    n = s // dil
    nb = -(-n // Q_BLOCK)
    n_pad = nb * Q_BLOCK

    def residue(t):
        return t.reshape(b, n, dil, h, dh).transpose(0, 2, 1, 3, 4)

    qr = jnp.pad(residue(q), ((0, 0), (0, 0), (0, n_pad - n), (0, 0), (0, 0)))
    qr = qr.reshape(b, dil, nb, Q_BLOCK, h, dh).astype(jnp.float32)

    def key_windows(t):
        tr = jnp.pad(residue(t), ((0, 0), (0, 0), (Q_BLOCK, n_pad - n), (0, 0), (0, 0)))
        tr = tr.reshape(b, dil, nb + 1, Q_BLOCK, h, dh)
        return jnp.concatenate([tr[:, :, :-1], tr[:, :, 1:]], axis=3).astype(jnp.float32)

    kw = key_windows(k)
    vw = key_windows(v)
    sc = jnp.einsum("brcqhd,brckhd->brchqk", qr, kw) * dh ** -0.5
    i = jnp.arange(Q_BLOCK)[:, None]
    j = jnp.arange(2 * Q_BLOCK)[None, :]
    dist = Q_BLOCK + i - j
    band = (dist >= 0) & (dist <= span)
    real = (jnp.arange(nb)[:, None, None] >= 1) | (j >= Q_BLOCK)[None]
    mask = band[None] & real
    sc = sc + bias[jnp.clip(dist, 0, span)].transpose(2, 0, 1)
    sc = jnp.where(mask[:, None], sc, -jnp.inf)
    m = jnp.max(sc, axis=-1, keepdims=True)
    p = jnp.exp(sc - m)
    den = jnp.sum(p, axis=-1)
    o = jnp.einsum("brchqk,brckhd->brcqhd", p / den[..., None], vw)
    lse = (m[..., 0] + jnp.log(den)).transpose(0, 1, 2, 4, 3)
    o = o.reshape(b, dil, n_pad, h, dh)[:, :, :n].transpose(0, 2, 1, 3, 4).reshape(b, s, h, dh)
    lse = lse.reshape(b, dil, n_pad, h)[:, :, :n].transpose(0, 2, 1, 3).reshape(b, s, h)
    return o, lse

def combine_dilations(outs, lses):
    w = jax.nn.softmax(jnp.stack(lses, axis=0), axis=0)
    return jnp.sum(w[..., None] * jnp.stack(outs, axis=0), axis=0)

def dilated_prompt(q, k, v, rel_bias):
    outs, lses = [], []
    for window, dil in DIL_CONFIGS:
        o, l = dilated_prompt_branch(q, k, v, dilation_bias(rel_bias, window, dil), window, dil)
        outs.append(o)
        lses.append(l)
    return combine_dilations(outs, lses)

def dilated_sample(q, k_ext, v_ext, n_buf, rel_bias):
    n_new = q.shape[1]
    dh = q.shape[-1]
    q32 = q.astype(jnp.float32)
    outs, lses = [], []
    for window, dil in DIL_CONFIGS:
        span = window // dil
        idx = n_buf + jnp.arange(n_new)[:, None] - jnp.arange(span + 1)[None, :] * dil
        valid = idx >= 0
        idx = jnp.maximum(idx, 0)
        kg = jnp.take(k_ext, idx, axis=1).astype(jnp.float32)
        vg = jnp.take(v_ext, idx, axis=1).astype(jnp.float32)
        sc = jnp.einsum("bqhd,bqjhd->bhqj", q32, kg) * dh ** -0.5
        sc = sc + dilation_bias(rel_bias, window, dil).T[:, None, :]
        sc = jnp.where(valid, sc, -jnp.inf)
        m = jnp.max(sc, axis=-1, keepdims=True)
        p = jnp.exp(sc - m)
        den = jnp.sum(p, axis=-1)
        outs.append(jnp.einsum("bhqj,bqjhd->bqhd", p / den[..., None], vg))
        lses.append((m[..., 0] + jnp.log(den)).transpose(0, 2, 1))
    return combine_dilations(outs, lses)

def merge_heads(o_fox, o_dil, g_fox, g_dil, w_out, dtype):
    lead = o_fox.shape[:-2]
    y = jnp.concatenate([rmsnorm(o_fox.reshape(*lead, W_FOX), g_fox),
                         rmsnorm(o_dil.reshape(*lead, W_DIL), g_dil)], axis=-1)
    return (y.astype(dtype) @ w_out).astype(dtype)

def peer(xn, w_query, sub_keys, u_tab, v_tab):
    lead = xn.shape[:-1]
    x2 = xn.reshape(-1, D_MODEL)
    t = x2.shape[0]
    nblk = -(-t // PEER_BLOCK)
    xb = jnp.pad(x2, ((0, nblk * PEER_BLOCK - t), (0, 0))).reshape(nblk, PEER_BLOCK, D_MODEL)
    half = D_QUERY // 2
    k1 = sub_keys[0].astype(jnp.float32)
    k2 = sub_keys[1].astype(jnp.float32)

    def block(xt):
        q = (xt @ w_query).astype(jnp.float32).reshape(PEER_BLOCK, PEER_HEADS, D_QUERY)
        s1 = jnp.einsum("thc,nc->thn", q[..., :half], k1)
        s2 = jnp.einsum("thc,nc->thn", q[..., half:], k2)
        v1, i1 = lax.top_k(s1, PEER_TOPK)
        v2, i2 = lax.top_k(s2, PEER_TOPK)
        cand = (v1[..., :, None] + v2[..., None, :]).reshape(PEER_BLOCK, PEER_HEADS, PEER_TOPK * PEER_TOPK)
        cidx = (i1[..., :, None] * N_KEYS + i2[..., None, :]).reshape(PEER_BLOCK, PEER_HEADS, PEER_TOPK * PEER_TOPK)
        top, pos = lax.top_k(cand, PEER_TOPK)
        eidx = jnp.take_along_axis(cidx, pos, axis=-1)
        g = jax.nn.softmax(top, axis=-1)
        hid = jnp.einsum("thkd,td->thk", u_tab[eidx].astype(jnp.float32), xt.astype(jnp.float32))
        a = g * jax.nn.gelu(hid, approximate=False)
        return jnp.einsum("thk,thkd->td", a, v_tab[eidx].astype(jnp.float32))

    out = lax.map(block, xb).reshape(nblk * PEER_BLOCK, D_MODEL)[:t]
    return out.reshape(*lead, D_MODEL).astype(xn.dtype)

def setup_inputs(seed: int = 0) -> dict:
    key = jax.random.key(seed)
    ks = jax.random.split(key, 24)
    f32 = jnp.float32
    n_pages = PAST_LEN // PAGE_SIZE
    n_used = DEC_BATCH * n_pages
    n_pool = n_used + max(1, n_used // 4)
    win_buf = min(MAX_WINDOW, PAST_LEN)

    def nrm(k, shape, scale):
        return jax.random.normal(k, shape, f32) * scale

    return {
        "x_prompt": nrm(ks[0], (BATCH, SEQ, D_MODEL), 1.0),
        "x_sample": nrm(ks[1], (DEC_BATCH, DEC_SEQ, D_MODEL), 1.0),
        "cache_k_fox": nrm(ks[2], (DEPTH, n_pool, PAGE_SIZE, N_HEADS_FOX, HEAD_DIM), 1.0),
        "cache_v_fox": nrm(ks[3], (DEPTH, n_pool, PAGE_SIZE, N_HEADS_FOX, HEAD_DIM), 1.0),
        "cache_logf_fox": jax.nn.log_sigmoid(FORGET_BIAS_INIT + nrm(ks[4], (DEPTH, n_pool, PAGE_SIZE, N_HEADS_FOX), 1.0)),
        "cache_k_win": nrm(ks[5], (DEPTH, DEC_BATCH, win_buf, N_HEADS_DIL, HEAD_DIM), 1.0),
        "cache_v_win": nrm(ks[6], (DEPTH, DEC_BATCH, win_buf, N_HEADS_DIL, HEAD_DIM), 1.0),
        "page_table": jax.random.permutation(ks[7], n_pool)[:n_used].reshape(DEC_BATCH, n_pages).astype(jnp.int32),
        "g_attn": 1.0 + nrm(ks[8], (DEPTH, D_MODEL), 0.02),
        "w_in": nrm(ks[9], (DEPTH, D_MODEL, N_IN), D_MODEL ** -0.5),
        "b_fgate": FORGET_BIAS_INIT + nrm(ks[10], (DEPTH, N_HEADS_FOX), 0.1),
        "g_out_fox": 1.0 + nrm(ks[11], (DEPTH, W_FOX), 0.02),
        "g_out_dil": 1.0 + nrm(ks[12], (DEPTH, W_DIL), 0.02),
        "w_out": nrm(ks[13], (DEPTH, D_MIX, D_MODEL), D_MIX ** -0.5),
        "rel_bias": nrm(ks[14], (N_BUCKETS, N_HEADS_DIL), 0.5),
        "g_ffn": 1.0 + nrm(ks[15], (DEPTH, D_MODEL), 0.02),
        "w_query": nrm(ks[16], (DEPTH, D_MODEL, PEER_HEADS * D_QUERY), D_MODEL ** -0.5),
        "sub_keys": nrm(ks[17], (DEPTH, 2, N_KEYS, D_QUERY // 2), (D_QUERY // 2) ** -0.5),
        "u_experts": nrm(ks[18], (DEPTH, N_EXPERTS, D_MODEL), D_MODEL ** -0.5),
        "v_experts": nrm(ks[19], (DEPTH, N_EXPERTS, D_MODEL), (PEER_HEADS * PEER_TOPK) ** -0.5),
        "g_final": 1.0 + nrm(ks[20], (D_MODEL,), 0.02),
    }

def reference(x_prompt, x_sample, cache_k_fox, cache_v_fox, cache_logf_fox, cache_k_win, cache_v_win,
              page_table, g_attn, w_in, b_fgate, g_out_fox, g_out_dil, w_out, rel_bias, g_ffn,
              w_query, sub_keys, u_experts, v_experts, g_final):
    hp = x_prompt
    hs = x_sample
    n_dec = x_sample.shape[0]
    win_prompt = min(MAX_WINDOW, x_prompt.shape[1])
    n_buf = cache_k_win.shape[2]
    kfp, vfp, lfp, kfs, vfs, lfs, kwp, vwp, kws, vws = [], [], [], [], [], [], [], [], [], []
    for l in range(DEPTH):
        qa, ka, va, qb, kb, vb, lf = split_projection(rmsnorm(hp, g_attn[l]), w_in[l], b_fgate[l])
        o_fox = fox_prompt(qa, ka, va, lf)
        o_dil = dilated_prompt(qb, kb, vb, rel_bias)
        hp = hp + merge_heads(o_fox, o_dil, g_out_fox[l], g_out_dil[l], w_out[l], hp.dtype)
        hp = hp + peer(rmsnorm(hp, g_ffn[l]), w_query[l], sub_keys[l], u_experts[l], v_experts[l])
        kfp.append(ka)
        vfp.append(va)
        lfp.append(lf)
        kwp.append(kb[:, -win_prompt:])
        vwp.append(vb[:, -win_prompt:])

        qa, ka, va, qb, kb, vb, lf = split_projection(rmsnorm(hs, g_attn[l]), w_in[l], b_fgate[l])
        k_past = cache_k_fox[l][page_table].reshape(n_dec, -1, N_HEADS_FOX, HEAD_DIM)
        v_past = cache_v_fox[l][page_table].reshape(n_dec, -1, N_HEADS_FOX, HEAD_DIM)
        lf_past = cache_logf_fox[l][page_table].reshape(n_dec, -1, N_HEADS_FOX)
        o_fox = fox_sample(qa, ka, va, lf, k_past, v_past, lf_past)
        o_dil = dilated_sample(qb, jnp.concatenate([cache_k_win[l], kb], axis=1),
                               jnp.concatenate([cache_v_win[l], vb], axis=1), n_buf, rel_bias)
        hs = hs + merge_heads(o_fox, o_dil, g_out_fox[l], g_out_dil[l], w_out[l], hs.dtype)
        hs = hs + peer(rmsnorm(hs, g_ffn[l]), w_query[l], sub_keys[l], u_experts[l], v_experts[l])
        kfs.append(ka)
        vfs.append(va)
        lfs.append(lf)
        kws.append(kb)
        vws.append(vb)

    y_prompt = rmsnorm(hp, g_final)
    y_sample = rmsnorm(hs, g_final)
    return (y_prompt, y_sample,
            jnp.stack(kfp), jnp.stack(vfp), jnp.stack(lfp),
            jnp.stack(kfs), jnp.stack(vfs), jnp.stack(lfs),
            jnp.stack(kwp), jnp.stack(vwp),
            jnp.stack(kws), jnp.stack(vws))


_drawn_inputs = setup_inputs


def setup_inputs(seed=0):
    import zlib

    import numpy as np

    out = dict(_drawn_inputs(seed))
    spreads = {}
    factors = {'g_out_fox': 16.925, 'g_out_dil': 17.678, 'g_ffn': 30.288, 'g_final': 8.715}
    for name, (base, spread) in spreads.items():
        noise = np.random.default_rng([zlib.crc32(name.encode()), seed]).standard_normal(out[name].shape)
        drawn = base * np.exp(spread * noise) if base else spread * noise
        out[name] = jnp.asarray(drawn.astype(out[name].dtype))
    for name, factor in factors.items():
        out[name] = (out[name] * factor).astype(out[name].dtype)
    return out
```

```python
import math

import numpy as np
import concourse.bass as bass
from concourse import mybir
from contextlib import ExitStack

F32 = mybir.dt.float32
F32R = mybir.dt.float32r
U32 = mybir.dt.uint32
ACT = mybir.ActivationFunctionType
ALU = mybir.AluOpType
AX = mybir.AxisListType

P = 128
D = 1024
KD = D // P
SEQ, DEC_B, DEC_S, PAST = 512, 8, 4, 256
PAGE = 128
NS = DEC_B * DEC_S
NT = SEQ + NS
TT = SEQ // P + 1
NTP = TT * P
HALF = NT // 2
HD, NH = 64, 8
PAIRS = NH
NBK = 32
NEG = -1.0e30
EPS = 1e-6
NK = 128
TOPK = 16
DIST = SEQ + P
SCALE8 = HD ** 0.5
CH = 68
NCH = NT // CH
GT = 4
NG = NK // GT


def rows(t):
    return P if t < TT - 1 else NS


def build(nc, A, O):
    ctx = ExitStack()
    persistent = ExitStack()

    def sem(name):
        return ctx.enter_context(nc.semaphore(name))

    def sb(stack, name, shape, dt=F32):
        return stack.enter_context(nc.sbuf_tensor(name, shape, dt))

    def ps(stack, name, shape):
        return stack.enter_context(nc.psum_tensor(name, shape, F32))

    bias_dram = nc.dram_tensor("bias_rows", (2 * NH, DIST), F32, kind="Internal").ap()
    tile_dram = nc.dram_tensor("bias_tiles", (2 * NH, P, SEQ), F32, kind="Internal").ap()
    cum_dram = nc.dram_tensor("cum_rows", (2 * NH, SEQ), F32, kind="Internal").ap()
    logf_dram = nc.dram_tensor("logf_rows", (NH, NT), F32, kind="Internal").ap()
    gate_dram = nc.dram_tensor("gate_matrix", (NCH, P, NK, CH), F32, kind="Internal").ap()
    h_dram = nc.dram_tensor("residual", (P, TT, D), F32, kind="Internal").ap()

    with ctx:
        ident = sb(ctx, "ident", [P, P])
        h = sb(persistent, "h", [P, TT, D])
        tiles_done = sem("tiles_done")
        passed = sem("passed")

        def settle(eng):
            eng.sem_inc(passed, 1)


        def norm_stage(tag, src, parts, gamma_dram, hi, lo, first_loads=None):
            W = D // parts
            with ExitStack() as st:
                gamma = sb(st, tag + "_gamma", [P, KD])
                ssq = sb(st, tag + "_ssq", [P, TT, parts])
                rstd = sb(st, tag + "_rstd", [P, TT, parts])
                sq = sb(st, tag + "_sq", [P, D])
                xs = sb(st, tag + "_xs", [P, 2, D])
                full = sb(st, tag + "_full", [P, 2, KD, P])
                tp = [ps(st, f"{tag}_tp{i}", [P, KD, P]) for i in range(2)]
                loaded, cleared, squared, meaned, rooted, inverted, scaled, turned, gained, split_hi, split_lo = (
                    sem(f"{tag}_{n}") for n in ("loaded", "cleared", "squared", "meaned", "rooted", "inverted",
                                                "scaled", "turned", "gained", "split_hi", "split_lo"))
                n_loads = 0 if first_loads is None else first_loads[0]
                block = st.enter_context(nc.Block())

                @block.sync
                def _(sp):
                    sp.dma_start(gamma[:], gamma_dram).then_inc(loaded, 16)
                    if first_loads is not None:
                        first_loads[1](sp, loaded)

                @block.gpsimd
                def _(pool):
                    nc.gpsimd.memset(hi[:, :, NT:].bitcast(F32), 0.0).then_inc(cleared, 1)
                    nc.gpsimd.memset(lo[:, :, NT:].bitcast(F32), 0.0).then_inc(cleared, 1)

                def split(act, t):
                    r = rows(t)
                    act.wait_ge(gained, t + 1)
                    nc.scalar.activation(hi[:, :, t * P:t * P + r], full[:, t % 2, :, :r], ACT.Copy).then_inc(split_hi, 1)

                @block.scalar
                def _(act):
                    act.wait_ge(loaded, 16 * (1 + n_loads))
                    act.wait_ge(meaned, 1)
                    for t in range(TT):
                        r = rows(t)
                        for g in range(parts):
                            if t or g:
                                act.wait_ge(squared, t * parts + g)
                            nc.scalar.activation(sq[:r, g * W:(g + 1) * W], src[:r, t, g * W:(g + 1) * W], ACT.Square,
                                                 accum_out=ssq[:r, t, g:g + 1]).then_inc(squared, 1)
                    act.wait_ge(meaned, 2)
                    nc.scalar.activation(rstd[:], ssq[:], ACT.Sqrt).then_inc(rooted, 1)
                    act.wait_ge(inverted, 1)
                    for t in range(TT):
                        r = rows(t)
                        if t >= 2:
                            act.wait_ge(turned, t - 1)
                        for g in range(parts):
                            nc.scalar.activation(xs[:r, t % 2, g * W:(g + 1) * W], src[:r, t, g * W:(g + 1) * W],
                                                 ACT.Copy, scale=ssq[:r, t, g:g + 1]).then_inc(scaled, 1)
                        if t >= 1:
                            split(act, t - 1)
                    split(act, TT - 1)

                @block.tensor
                def _(pe):
                    for t in range(TT):
                        r = rows(t)
                        pe.wait_ge(scaled, parts * (t + 1))
                        if t >= 2:
                            pe.wait_ge(gained, t - 1)
                        for k in range(KD):
                            last = nc.tensor.transpose(tp[t % 2][:, k, :r], xs[:r, t % 2, k * P:(k + 1) * P], ident[:r, :r])
                        last.then_inc(turned, 1)

                @block.vector
                def _(dve):
                    nc.vector.memset(ssq[:], 1.0).then_inc(meaned, 1)
                    dve.wait_ge(squared, TT * parts)
                    nc.vector.tensor_scalar(ssq[:], ssq[:], 1.0 / W, EPS, ALU.mult, ALU.add).then_inc(meaned, 1)
                    dve.wait_ge(rooted, 1)
                    nc.vector.reciprocal(ssq[:], rstd[:]).then_inc(inverted, 1)
                    for t in range(TT):
                        r = rows(t)
                        dve.wait_ge(turned, t + 1)
                        if t >= 2:
                            dve.wait_ge(split_hi, t - 1)
                            dve.wait_ge(split_lo, t - 1)
                        nc.vector.tensor_tensor(full[:, t % 2, :, :r], tp[t % 2][:, :, :r],
                                                gamma[:].unsqueeze(2).broadcast_to([P, KD, r]), ALU.mult).then_inc(gained, 1)
                        dve.wait_ge(split_hi, t + 1)
                        nc.vector.tensor_tensor(lo[:, :, t * P:t * P + r], full[:, t % 2, :, :r],
                                                hi[:, :, t * P:t * P + r].bitcast(F32), ALU.subtract).then_inc(split_lo, 1)

        def mm3(out, a_hi, a_lo, b_hi, b_lo, first, last):
            nc.tensor.matmul(out, a_hi, b_hi, start=first, stop=False)
            nc.tensor.matmul(out, a_hi, b_lo, start=False, stop=False)
            return nc.tensor.matmul(out, a_lo, b_hi, start=False, stop=last)

        def token_rows_product(st, tag, xhi, xlo, w_dram, w_tiles, evacuate):
            CW = 256
            w = sb(st, tag + "_w", [P, 2, KD, CW])
            whi = sb(st, tag + "_whi", [P, 2, KD, CW], F32R)
            wlo = sb(st, tag + "_wlo", [P, 2, KD, CW], F32R)
            acc = [ps(st, f"{tag}_acc{i}", [P, CW]) for i in range(2)]
            wld = [sem(f"{tag}_wld{u}") for u in range(2)]
            hi_done, lo_done, mm_done, out_done = (sem(f"{tag}_{n}") for n in ("hi_done", "lo_done", "mm_done", "out_done"))
            NP = w_tiles // 2

            def on_sync(sp):
                with sp.Fori(0, NP) as j:
                    for u in range(2):
                        sp.wait_ge(lo_done, 2 * j + u + 1)
                        sp.dma_start(w[:, u], w_dram[2 * j + u]).then_inc(wld[u], 16)

            def on_scalar(act):
                with act.Fori(0, NP) as j:
                    for u in range(2):
                        act.wait_ge(wld[u], 16 * (j + 1))
                        act.wait_ge(mm_done, (2 * j + u + 1) * TT)
                        nc.scalar.activation(whi[:, u], w[:, u], ACT.Copy).then_inc(hi_done, 1)

            def on_vector(dve):
                dve.sem_inc(lo_done, 2)
                dve.sem_inc(out_done, 2)

                def split(chunk, u):
                    dve.wait_ge(hi_done, chunk + 1)
                    nc.vector.tensor_tensor(wlo[:, u], w[:, u], whi[:, u].bitcast(F32), ALU.subtract).then_inc(lo_done, 1)

                with dve.Fori(0, NP) as j:
                    for u in range(2):
                        split(2 * j + u, u)
                        for t in range(TT):
                            dve.wait_ge(mm_done, (2 * j + u) * TT + t + 2 * TT + 1)
                            evacuate(t, 2 * j + u, acc[(u * TT + t) % 2]).then_inc(out_done, 1)

            def on_tensor(pe):
                pe.sem_inc(mm_done, 2 * TT)
                with pe.Fori(0, NP) as j:
                    for u in range(2):
                        pe.wait_ge(lo_done, 2 * j + u + 3)
                        for t in range(TT):
                            pe.wait_ge(out_done, (2 * j + u) * TT + t + 1)
                            for k in range(KD):
                                last = mm3(acc[(u * TT + t) % 2][:], xhi[:, k, t * P:(t + 1) * P], xlo[:, k, t * P:(t + 1) * P],
                                           whi[:, u, k], wlo[:, u, k], k == 0, k == KD - 1)
                            last.then_inc(mm_done, 1)

            return on_sync, on_scalar, on_vector, on_tensor

        with ExitStack() as st:
            onehot = sb(st, "onehot", [NBK + 2, DIST])
            relw = sb(st, "relw", [NBK + 2, 2 * NH])
            brow = sb(st, "brow", [2 * NH, DIST])
            zrow = sb(st, "zrow", [NH, SEQ])
            bp = ps(st, "bp", [2 * NH, DIST])
            t_ld, t_clr, t_mm, t_ev, t_out = (sem("t_" + n) for n in ("ld", "clr", "mm", "ev", "out"))
            block = st.enter_context(nc.Block())

            @block.sync
            def _(sp):
                sp.dma_start(ident[:], A["ident"]).then_inc(t_ld, 16)
                sp.dma_start(onehot[:], A["bucket_onehot"]).then_inc(t_ld, 16)
                sp.wait_ge(t_clr, 1)
                sp.dma_start(relw[:NBK, NH:], A["rel_bias"]).then_inc(t_ld, 16)
                sp.dma_start(relw[NBK:, :], A["row_kind"]).then_inc(t_ld, 16)
                sp.wait_ge(t_ev, 2)
                sp.dma_start(bias_dram, brow[:]).then_inc(t_out, 16)
                sp.wait_ge(t_clr, 2)
                sp.dma_start(cum_dram[NH:], zrow[:]).then_inc(t_out, 16)
                sp.wait_ge(t_out, 32)
                diagonals = bass.AP(bias_dram.tensor, P - 1, [[DIST, 2 * NH], [-1, P], [1, SEQ]])
                sp.dma_start(tile_dram, diagonals).then_inc(tiles_done, 16)

            @block.vector
            def _(dve):
                nc.vector.memset(relw[:], 0.0).then_inc(t_clr, 1)
                nc.vector.memset(zrow[:], 0.0).then_inc(t_clr, 1)
                dve.wait_ge(t_mm, 2)
                nc.vector.tensor_scalar(brow[:, :SEQ], bp[:, :SEQ], SCALE8, None, ALU.mult).then_inc(t_ev, 1)
                nc.vector.tensor_scalar(brow[:, SEQ:], bp[:, SEQ:], SCALE8, None, ALU.mult).then_inc(t_ev, 1)

            @block.tensor
            def _(pe):
                pe.wait_ge(t_ld, 64)
                nc.tensor.matmul(bp[:, :SEQ], relw[:], onehot[:, :SEQ], start=True, stop=True).then_inc(t_mm, 1)
                nc.tensor.matmul(bp[:, SEQ:], relw[:], onehot[:, SEQ:], start=True, stop=True).then_inc(t_mm, 1)

        attn = ExitStack()
        qkT = sb(attn, "qkT", [P, 2 * PAIRS, NT])
        v = sb(attn, "v", [P, TT, D])

        def load_x(sp, loaded):
            sp.dma_start(h[:, 0:TT - 1, :], A["x_prompt"].rearrange("(t p) d -> p t d", p=P)).then_inc(loaded, 16)
            sp.dma_start(h[:NS, TT - 1, :], A["x_sample"]).then_inc(loaded, 16)

        proj = ExitStack()
        xhi = sb(proj, "xhi", [P, KD, NTP], F32R)
        xlo = sb(proj, "xlo", [P, KD, NTP], F32R)
        norm_stage("na", h, 1, A["g_attn"], xhi, xlo, (2, load_x))

        with ExitStack() as st:
            w = sb(st, "pw", [P, 2, KD, P])
            whi = sb(st, "pwhi", [P, 2, KD, P], F32R)
            wlo = sb(st, "pwlo", [P, 2, KD, P], F32R)
            kz = sb(st, "kz", [P, NT])
            kn = sb(st, "kn", [P, TT, P])
            zp = [ps(st, f"zp{i}", [P, 2, SEQ]) for i in range(2)]
            kp = ps(st, "kp", [P, 8, P])
            wld = [sem(f"p_wld{u}") for u in range(2)]
            hi_done, lo_done, mm_done, ev_done, kt_done, kn_done, k_out = (
                sem("p_" + n) for n in ("hi_done", "lo_done", "mm_done", "ev_done", "kt_done", "kn_done", "k_out"))
            kcopied = sem("p_kcopied")
            kn_free = sem("p_kn_free")
            block = st.enter_context(nc.Block())
            k_outs = ((O["kfp"], O["kfs"]), (O["kwp"], O["kws"]))

            @block.sync
            def _(sp):
                for kind in range(2):
                    with sp.Fori(0, NH // 2) as j:
                        for u in range(2):
                            n = kind * NH + 2 * j + u
                            sp.wait_ge(lo_done, n + 1)
                            sp.dma_start(w[:, u], A["w_qk"][n]).then_inc(wld[u], 16)

            @block.scalar
            def _(act):
                act.sem_inc(ev_done, 2)
                for kind in range(2):
                    with act.Fori(0, NH // 2) as j:
                        for u in range(2):
                            n = kind * NH + 2 * j + u
                            act.wait_ge(wld[u], 16 * (kind * (NH // 2) + j + 1))
                            act.wait_ge(mm_done, n + 1)
                            nc.scalar.activation(whi[:, u], w[:, u], ACT.Copy).then_inc(hi_done, 1)
                            act.wait_ge(mm_done, n + 3)
                            if u == 0:
                                nc.scalar.activation(qkT[:, n, :].rearrange("p (a b) -> p a b", a=2),
                                                     zp[u][:, :, :HALF], ACT.Copy).then_inc(ev_done, 1)
                            else:
                                act.wait_ge(kt_done, kind * (NH // 2) + j + 1)
                                act.wait_ge(kcopied, kind * (NH // 2) + j + 1)
                                nc.scalar.activation(kz[:].rearrange("p (a b) -> p a b", a=2),
                                                     zp[u][:, :, :HALF], ACT.Copy).then_inc(ev_done, 1)

            @block.vector
            def _(dve):
                dve.sem_inc(lo_done, 2)
                dve.sem_inc(kn_done, 1)
                dve.sem_inc(kcopied, 1)
                for kind in range(2):
                    with dve.Fori(0, NH // 2) as j:
                        for u in range(2):
                            n = kind * NH + 2 * j + u
                            m = kind * (NH // 2) + j
                            dve.wait_ge(hi_done, n + 1)
                            nc.vector.tensor_tensor(wlo[:, u], w[:, u], whi[:, u].bitcast(F32), ALU.subtract).then_inc(lo_done, 1)
                            if u == 1:
                                dve.wait_ge(ev_done, n + 3)
                                nc.vector.tensor_copy(qkT[:, n, :], kz[:]).then_inc(kcopied, 1)
                                dve.wait_ge(kt_done, m + 2)
                                dve.wait_ge(kn_free, m + 1)
                                nc.vector.tensor_copy(kn[:, 0:TT - 1], kp[:, 0:TT - 1])
                                nc.vector.tensor_copy(kn[:NS, TT - 1], kp[:NS, TT - 1]).then_inc(kn_done, 1)

            @block.tensor
            def _(pe):
                pe.sem_inc(mm_done, 2)
                pe.sem_inc(kt_done, 1)
                for kind in range(2):
                    with pe.Fori(0, NH // 2) as j:
                        for u in range(2):
                            n = kind * NH + 2 * j + u
                            m = kind * (NH // 2) + j
                            pe.wait_ge(lo_done, n + 3)
                            pe.wait_ge(ev_done, n + 1)
                            for k in range(KD):
                                for f in range(2):
                                    last = mm3(zp[u][:, f, :HALF], whi[:, u, k], wlo[:, u, k],
                                               xhi[:, k, f * HALF:(f + 1) * HALF], xlo[:, k, f * HALF:(f + 1) * HALF],
                                               k == 0, k == KD - 1)
                            last.then_inc(mm_done, 1)
                            if u == 1:
                                pe.wait_ge(ev_done, n + 3)
                                pe.wait_ge(kn_done, m + 1)
                                for t in range(TT):
                                    r = rows(t)
                                    last = nc.tensor.transpose(kp[:r, t, :], kz[:, t * P:t * P + r], ident[:])
                                last.then_inc(kt_done, 1)

            @block.gpsimd
            def _(pool):
                pool.sem_inc(kn_free, 1)
                for kind in range(2):
                    prompt_out, sample_out = k_outs[kind]
                    with pool.Fori(0, NH // 2) as j:
                        m = kind * (NH // 2) + j
                        pool.wait_ge(kn_done, m + 2)
                        pool.dma_start(prompt_out.rearrange("(t p) (c n) -> c p t n", p=P, n=P)[j], kn[:, 0:TT - 1]).then_inc(k_out, 16)
                        pool.dma_start(sample_out.rearrange("t (c n) -> c t n", n=P)[j], kn[:NS, TT - 1]).then_inc(k_out, 16)
                        pool.wait_ge(k_out, 32 * m + 32)
                        pool.sem_inc(kn_free, 1)
                pool.wait_ge(k_out, 32 * NH)

        with ExitStack() as st:
            def keep_v(t, chunk, acc):
                return nc.vector.tensor_copy(v[:, t, bass.ds(chunk * 256, 256)], acc[:])

            on_sync, on_scalar, on_vector, on_tensor = token_rows_product(st, "pv", xhi, xlo, A["w_v"], 4, keep_v)
            wf = sb(st, "wf", [P, KD, NH])
            bf = sb(st, "bf", [NH, 1])
            gz, ga, ge, gu, gl, gd, gw = (sb(st, "g" + n, [NH, NT]) for n in ("z", "a", "e", "u", "l", "d", "w"))
            logf = sb(st, "logf", [NH, NT])
            cum = sb(st, "cum", [NH, SEQ])
            lf = sb(st, "lf", [P, TT, NH])
            zf = ps(st, "zf", [NH, 2, SEQ])
            lp = ps(st, "lp", [P, TT, NH])
            f_ld, f_mm, f_act, f_dve, f_tr, f_out = (sem("f_" + n) for n in ("ld", "mm", "act", "dve", "tr", "out"))
            block = st.enter_context(nc.Block())

            @block.sync
            def _(sp):
                sp.dma_start(wf[:], A["w_f"]).then_inc(f_ld, 16)
                sp.dma_start(bf[:], A["b_f"]).then_inc(f_ld, 16)
                on_sync(sp)
                sp.wait_ge(f_dve, 10)
                sp.dma_start(logf_dram, logf[:]).then_inc(f_out, 16)
                sp.dma_start(cum_dram[:NH], cum[:]).then_inc(f_out, 16)
                sp.wait_ge(f_dve, 11)
                sp.dma_start(O["lfp"].rearrange("(t p) h -> p t h", p=P), lf[:, 0:TT - 1]).then_inc(f_out, 16)
                sp.dma_start(O["lfs"], lf[:NS, TT - 1]).then_inc(f_out, 16)
                for kind, (prompt_out, sample_out) in enumerate(((O["vfp"], O["vfs"]), (O["vwp"], O["vws"]))):
                    sp.dma_start(prompt_out.rearrange("(t p) n -> p t n", p=P),
                                 v[:, 0:TT - 1, kind * 512:(kind + 1) * 512]).then_inc(f_out, 16)
                    sp.dma_start(sample_out, v[:NS, TT - 1, kind * 512:(kind + 1) * 512]).then_inc(f_out, 16)
                sp.wait_ge(f_out, 128)

            @block.scalar
            def _(act):
                on_scalar(act)
                act.wait_ge(f_ld, 32)
                act.wait_ge(f_mm, 1)
                nc.scalar.activation(gz[:].rearrange("p (a b) -> p a b", a=2), zf[:, :, :HALF], ACT.Identity,
                                     bias=bf[:]).then_inc(f_act, 1)
                act.wait_ge(f_act, 1)
                nc.scalar.activation(ga[:], gz[:], ACT.Abs).then_inc(f_act, 1)
                act.wait_ge(f_act, 2)
                nc.scalar.activation(ge[:], ga[:], ACT.Exp, scale=-1.0).then_inc(f_act, 1)
                act.wait_ge(f_dve, 1)
                nc.scalar.activation(gl[:], gu[:], ACT.Ln).then_inc(f_act, 1)

            @block.vector
            def _(dve):
                on_vector(dve)
                count = [0]

                def step(ins):
                    count[0] += 1
                    ins.then_inc(f_dve, 1)
                    dve.wait_ge(f_dve, count[0])

                dve.wait_ge(f_act, 3)
                step(nc.vector.tensor_scalar(gu[:], ge[:], 1.0, None, ALU.add))
                step(nc.vector.tensor_scalar(gd[:], gu[:], -1.0, None, ALU.add))
                step(nc.vector.tensor_scalar(gw[:], gd[:], 0.0, None, ALU.is_equal))
                step(nc.vector.tensor_tensor(gd[:], gd[:], gw[:], ALU.add))
                step(nc.vector.reciprocal(gd[:], gd[:]))
                dve.wait_ge(f_act, 4)
                step(nc.vector.tensor_tensor(gw[:], gl[:], gw[:], ALU.add))
                step(nc.vector.tensor_tensor(gd[:], gd[:], gw[:], ALU.mult))
                step(nc.vector.tensor_tensor(gd[:], gd[:], ge[:], ALU.mult))
                step(nc.vector.scalar_tensor_tensor(logf[:], gz[:], 0.0, gd[:], ALU.min, ALU.subtract))
                nc.vector.memset(ga[:], 1.0).then_inc(f_tr, 1)
                dve.wait_ge(f_tr, 1)
                nc.vector.tensor_tensor_scan(cum[:], ga[:, :SEQ], logf[:, :SEQ], 0.0, ALU.mult, ALU.add).then_inc(f_tr, 1)
                dve.wait_ge(f_tr, 2)
                step(nc.vector.tensor_scalar(cum[:], cum[:], -SCALE8, None, ALU.mult))
                dve.wait_ge(f_mm, 2)
                nc.vector.tensor_copy(lf[:, 0:TT - 1], lp[:, 0:TT - 1])
                step(nc.vector.tensor_copy(lf[:NS, TT - 1], lp[:NS, TT - 1]))

            @block.tensor
            def _(pe):
                on_tensor(pe)
                pe.wait_ge(f_ld, 32)
                for f in range(2):
                    cols = slice(f * HALF, (f + 1) * HALF)
                    for k in range(KD):
                        nc.tensor.matmul(zf[:, f, :HALF], wf[:, k], xhi[:, k, cols].bitcast(F32), start=k == 0, stop=False)
                        last = nc.tensor.matmul(zf[:, f, :HALF], wf[:, k], xlo[:, k, cols].bitcast(F32),
                                                start=False, stop=k == KD - 1)
                last.then_inc(f_mm, 1)
                pe.wait_ge(f_dve, 9)
                for t in range(TT):
                    r = rows(t)
                    last = nc.tensor.transpose(lp[:r, t], logf[:, t * P:t * P + r], ident[:NH, :NH])
                last.then_inc(f_mm, 1)
        proj.close()

        o = sb(attn, "o", [P, TT, D])
        with ExitStack() as st:
            qa = sb(st, "qa", [HD + 1, 2, SEQ])
            ka = sb(st, "ka", [HD + 1, 2, SEQ])
            vh = sb(st, "vh", [P, 2, TT - 1, HD])
            bt = sb(st, "bt", [P, 2, SEQ])
            L = sb(st, "L", [P, 2, SEQ])
            negm = sb(st, "negm", [P, 2])
            E = sb(st, "E", [P, 2, SEQ])
            ET = sb(st, "ET", [P, 2, 4, P])
            den = sb(st, "den", [P, 2, 4])
            rden = sb(st, "rden", [P, 2, 4])
            S = [ps(st, f"S{i}", [P, SEQ]) for i in range(2)]
            TP = [ps(st, f"TP{i}", [P, 4, P]) for i in range(2)]
            OP = [ps(st, f"OP{i}", [P, 4, HD]) for i in range(2)]
            stg = [sem(f"a_stg{u}") for u in range(2)]
            s_mm, l_done, e_done, t_mm2, t_ev2, pv_mm, r_done, o_ev, one = (
                sem("a_" + n) for n in ("s_mm", "l_done", "e_done", "t_mm", "t_ev", "pv_mm", "r_done", "o_ev", "one"))
            block = st.enter_context(nc.Block())
            QB = TT - 1
            steps = [(u, qb) for u in range(2) for qb in range(QB)]

            @block.sync
            def _(sp):
                sp.wait_ge(tiles_done, 16)
                with sp.Fori(0, PAIRS) as j:
                    for u in range(2):
                        sp.wait_ge(o_ev, 2 * j + u + 1)
                        sp.dma_start(qa[:HD, u, :], qkT[u * HD:(u + 1) * HD, 2 * j, :SEQ]).then_inc(stg[u], 16)
                        sp.dma_start(ka[:HD, u, :], qkT[u * HD:(u + 1) * HD, 2 * j + 1, :SEQ]).then_inc(stg[u], 16)
                        sp.dma_start(ka[HD:HD + 1, u, :], cum_dram[bass.ds(2 * j + u, 1)]).then_inc(stg[u], 16)
                        sp.dma_start(vh[:, u], v[:, 0:QB, bass.ds(j * P + u * HD, HD)]).then_inc(stg[u], 16)
                        sp.dma_start(bt[:, u], tile_dram[2 * j + u]).then_inc(stg[u], 16)

            @block.tensor
            def _(pe):
                pe.sem_inc(t_mm2, 2)
                pe.sem_inc(pv_mm, 2)
                pe.wait_ge(one, 1)
                with pe.Fori(0, PAIRS) as j:
                    def scores(i):
                        u, qb = steps[i]
                        n = (qb + 1) * P
                        if qb == 0:
                            pe.wait_ge(stg[u], 80 * (j + 1))
                        pe.wait_ge(l_done, 8 * j + i + 1)
                        nc.tensor.matmul(S[i % 2][:, :n], qa[:, u, qb * P:(qb + 1) * P], ka[:, u, :n],
                                         start=True, stop=True).then_inc(s_mm, 1)

                    scores(0)
                    for i, (u, qb) in enumerate(steps):
                        if i + 1 < len(steps):
                            scores(i + 1)
                        pe.wait_ge(e_done, 8 * j + i + 3)
                        pe.wait_ge(t_ev2, 8 * j + i + 1)
                        for b in range(qb + 1):
                            last = nc.tensor.transpose(TP[i % 2][:, b], E[:, i % 2, b * P:(b + 1) * P], ident[:])
                        last.then_inc(t_mm2, 1)
                        pe.wait_ge(t_ev2, 8 * j + i + 3)
                        if qb == 0:
                            pe.wait_ge(o_ev, 2 * j + u + 1)
                        for b in range(qb + 1):
                            last = nc.tensor.matmul(OP[u][:, qb], ET[:, i % 2, b], vh[:, u, b],
                                                    start=b == 0, stop=b == qb)
                        last.then_inc(pv_mm, 1)

            @block.vector
            def _(dve):
                dve.sem_inc(l_done, 2)
                dve.sem_inc(t_ev2, 2)
                dve.sem_inc(o_ev, 2)
                nc.vector.memset(qa[HD:HD + 1], 1.0).then_inc(one, 1)
                with dve.Fori(0, PAIRS) as j:
                    def logits(i):
                        u, qb = steps[i]
                        n = (qb + 1) * P
                        dve.wait_ge(e_done, 8 * j + i + 1)
                        dve.wait_ge(s_mm, 8 * j + i + 1)
                        settle(dve)
                        nc.vector.tensor_tensor_reduce(
                            out=L[:, i % 2, :n], in0=S[i % 2][:, :n], in1=bt[:, u, SEQ - n:], scale=-1.0 / SCALE8,
                            scalar=3.0e38, op0=ALU.add, op1=ALU.min, accum_out=negm[:, i % 2:i % 2 + 1]).then_inc(l_done, 1)

                    logits(0)
                    for i, (u, qb) in enumerate(steps):
                        if i + 1 < len(steps):
                            logits(i + 1)
                        dve.wait_ge(t_mm2, 8 * j + i + 3)
                        dve.wait_ge(pv_mm, 8 * j + i + 1)
                        nc.vector.tensor_copy(ET[:, i % 2, :qb + 1], TP[i % 2][:, :qb + 1]).then_inc(t_ev2, 1)
                        if qb == QB - 1:
                            nc.vector.reciprocal(rden[:, u], den[:, u]).then_inc(r_done, 1)
                            dve.wait_ge(r_done, 2 * j + u + 1)
                            dve.wait_ge(pv_mm, 8 * j + i + 3)
                            nc.vector.tensor_tensor(o[:, 0:QB, bass.ds(j * P + u * HD, HD)], OP[u][:],
                                                    rden[:, u].unsqueeze(2).broadcast_to([P, QB, HD]),
                                                    ALU.mult).then_inc(o_ev, 1)

            @block.scalar
            def _(act):
                act.sem_inc(e_done, 2)
                with act.Fori(0, PAIRS) as j:
                    for i, (u, qb) in enumerate(steps):
                        n = (qb + 1) * P
                        if qb == 0:
                            act.wait_ge(o_ev, 2 * j + u + 1)
                        act.wait_ge(l_done, 8 * j + i + 3)
                        act.wait_ge(t_mm2, 8 * j + i + 1)
                        nc.scalar.activation(E[:, i % 2, :n], L[:, i % 2, :n], ACT.Exp, bias=negm[:, i % 2:i % 2 + 1],
                                             scale=-1.0, accum_out=den[:, u, qb:qb + 1]).then_inc(e_done, 1)

        NPG = PAST // PAGE
        GB = 4
        UC = PAST + NS
        with ExitStack() as st:
            qd = sb(st, "qd", [P, 2, 4, DEC_B, NS])
            kc = sb(st, "kc", [P, DEC_B, 4, PAST])
            vc = sb(st, "vc", [P, DEC_B, NPG, 512])
            pt = sb(st, "pt", [1, DEC_B * NPG], mybir.dt.int32)
            T = sb(st, "T", [P, 4, UC])
            lg = sb(st, "lg", [P, 2, PAST + DEC_S])
            ones = sb(st, "sones", [P, PAST + DEC_S])
            newmask = sb(st, "newmask", [P, DEC_S])
            hmask = sb(st, "hmask", [P, NH])
            sel = sb(st, "sel", [P, 2, NS])
            L = sb(st, "sL", [P, 2, UC])
            E = sb(st, "sE", [P, 2, UC])
            ET = sb(st, "sET", [P, 2, NPG + 1, P])
            negm = sb(st, "snegm", [P, 4])
            den = sb(st, "sden", [P, 4])
            rden = sb(st, "srden", [P, 4])
            Om = sb(st, "sOm", [P, 2, 512])
            S = [ps(st, f"sS{i}", [P, UC]) for i in range(2)]
            TP = [ps(st, f"sTP{i}", [P, NPG + 1, P]) for i in range(2)]
            OP = [ps(st, f"sOP{i}", [P, 512]) for i in range(2)]
            OS = [ps(st, f"sOS{i}", [NS, 512]) for i in range(2)]
            names = ("pt", "consts", "clear", "lg", "dil", "scan", "T", "qd", "s_mm", "l", "e", "t_mm", "et", "pv",
                     "r", "om", "os", "oev")
            s = {n: sem("s_" + n) for n in names}
            kld = [sem(f"s_kld{g}") for g in range(DEC_B // GB)]
            vld = [sem(f"s_vld{g}") for g in range(DEC_B // GB)]
            block = st.enter_context(nc.Block())
            n_pool = A["k_pages"].shape[0]
            units = [(kind, g) for kind in range(2) for g in range(DEC_B // GB)]

            @block.sync
            def _(sp):
                sp.dma_start(pt[:], A["page_table"]).then_inc(s["pt"], 16)
                sp.dma_start(hmask[:], A["head_mask"]).then_inc(s["consts"], 16)
                sp.dma_start(sel[:], A["row_select"]).then_inc(s["consts"], 16)
                sp.wait_ge(s["pt"], 16)
                for b in range(DEC_B):
                    g, bi = b // GB, b % GB
                    for i in range(NPG):
                        page = sp.value_load(pt[0:1, b * NPG + i:b * NPG + i + 1], min_val=0, max_val=n_pool - 1)
                        sp.dma_start(kc[:, b, :, i * PAGE:(i + 1) * PAGE], A["k_pages"][page]).then_inc(kld[b // GB], 16)
                        sp.dma_start(vc[:, b, i], A["v_pages"][page]).then_inc(vld[b // GB], 16)
                        src = A["logf_pages"][page].unsqueeze(1).broadcast_to([NH, DEC_S, PAGE])
                        sp.dma_start(lg[NS * bi:NS * (bi + 1), g, i * PAGE:(i + 1) * PAGE], src).then_inc(s["lg"], 16)
                    new = bass.AP(logf_dram.tensor, SEQ + b * DEC_S, [[NT, NH], [0, DEC_S], [1, DEC_S]])
                    sp.dma_start(lg[NS * bi:NS * (bi + 1), g, PAST:], new).then_inc(s["lg"], 16)
                for b in range(DEC_B):
                    sp.wait_ge(s["s_mm"], b // GB + 1)
                    sp.dma_start(kc[:, b], A["k_win"][b]).then_inc(kld[b // GB], 16)
                for b in range(DEC_B):
                    sp.wait_ge(s["pv"], b // GB + 1)
                    sp.dma_start(vc[:, b], A["v_win"][b].rearrange("(i p) n -> p i n", p=P)).then_inc(vld[b // GB], 16)

            @block.gpsimd
            def _(pool):
                pool.wait_ge(s["clear"], 2)
                for g in range(DEC_B // GB):
                    for bi in range(GB):
                        rws = slice(NS * bi, NS * (bi + 1))
                        past = bass.AP(bias_dram.tensor, NH * DIST + SEQ - 1 - PAST, [[DIST, NH], [-1, DEC_S], [1, PAST]])
                        pool.dma_start(T[rws, 2 + g, :PAST], past).then_inc(s["dil"], 16)
                        new = bass.AP(bias_dram.tensor, NH * DIST + SEQ - 1, [[DIST, NH], [-1, DEC_S], [1, DEC_S]])
                        c0 = PAST + DEC_S * (GB * g + bi)
                        pool.dma_start(T[rws, 2 + g, c0:c0 + DEC_S], new).then_inc(s["dil"], 16)
                for bi in range(GB):
                    future = bass.AP(bias_dram.tensor, SEQ - 1, [[DIST, NH], [-1, DEC_S], [1, DEC_S]])
                    pool.dma_start(newmask[NS * bi:NS * (bi + 1)], future).then_inc(s["dil"], 16)

            @block.vector
            def _(dve):
                nc.vector.memset(qd[:], 0.0).then_inc(s["clear"], 1)
                nc.vector.memset(T[:], NEG).then_inc(s["clear"], 1)
                nc.vector.memset(ET[:], 0.0).then_inc(s["clear"], 1)
                nc.vector.memset(ones[:], 1.0).then_inc(s["clear"], 1)
                dve.wait_ge(s["clear"], 4)
                for kind in range(2):
                    for c in range(4):
                        for u in range(2):
                            hh = 2 * c + u
                            src = qkT[u * HD:(u + 1) * HD, 2 * (kind * 4 + c), SEQ:].rearrange("p (b q) -> p b q", b=DEC_B)
                            nc.vector.tensor_copy(qd[u * HD:(u + 1) * HD, kind, c, :, hh * DEC_S:(hh + 1) * DEC_S],
                                                  src).then_inc(s["qd"], 1)
                dve.wait_ge(s["lg"], 16 * DEC_B * (NPG + 1))
                dve.wait_ge(s["consts"], 32)
                dve.wait_ge(s["dil"], 16 * 5 * GB)
                for g in range(2):
                    nc.vector.tensor_tensor_scan(lg[:, g], ones[:], lg[:, g], 0.0, ALU.mult, ALU.add).then_inc(s["scan"], 1)
                for g in range(2):
                    dve.wait_ge(s["scan"], g + 1)
                    nc.vector.tensor_scalar(T[:, g, :PAST], lg[:, g, :PAST], -SCALE8, None, ALU.mult).then_inc(s["T"], 1)
                    for bi in range(GB):
                        rws = slice(NS * bi, NS * (bi + 1))
                        c0 = PAST + DEC_S * (GB * g + bi)
                        nc.vector.scalar_tensor_tensor(T[rws, g, c0:c0 + DEC_S], lg[rws, g, PAST:], -SCALE8, newmask[rws],
                                                       ALU.mult, ALU.add).then_inc(s["T"], 1)

                def logits(i):
                    if i == 0:
                        dve.wait_ge(s["T"], 2 * (GB + 1))
                    if i >= 2:
                        dve.wait_ge(s["e"], i - 1)
                    dve.wait_ge(s["s_mm"], i + 1)
                    nc.vector.tensor_tensor_reduce(
                        out=L[:, i % 2], in0=S[i % 2][:], in1=T[:, i], scale=-1.0 / SCALE8, scalar=3.0e38,
                        op0=ALU.add, op1=ALU.min, accum_out=negm[:, i:i + 1]).then_inc(s["l"], 1)

                logits(0)
                for i in range(4):
                    if i + 1 < 4:
                        logits(i + 1)
                    dve.wait_ge(s["t_mm"], i + 1)
                    if i >= 2:
                        dve.wait_ge(s["pv"], i - 1)
                    nc.vector.tensor_copy(ET[:, i % 2, :NPG], TP[i % 2][:, :NPG])
                    nc.vector.tensor_copy(ET[:NS, i % 2, NPG], TP[i % 2][:NS, NPG]).then_inc(s["et"], 1)
                    nc.vector.reciprocal(rden[:, i:i + 1], den[:, i:i + 1]).then_inc(s["r"], 1)
                    dve.wait_ge(s["r"], i + 1)
                    dve.wait_ge(s["pv"], i + 1)
                    if i >= 2:
                        dve.wait_ge(s["os"], i - 1)
                    nc.vector.scalar_tensor_tensor(
                        Om[:, i % 2].rearrange("p (h d) -> p h d", h=NH), OP[i % 2][:].rearrange("p (h d) -> p h d", h=NH),
                        rden[:, i:i + 1], hmask[:].unsqueeze(2).broadcast_to([P, NH, HD]), ALU.mult, ALU.mult).then_inc(s["om"], 1)

            @block.scalar
            def _(act):
                for i in range(4):
                    act.wait_ge(s["l"], i + 1)
                    if i >= 2:
                        act.wait_ge(s["t_mm"], i - 1)
                    nc.scalar.activation(E[:, i % 2], L[:, i % 2], ACT.Exp, bias=negm[:, i:i + 1], scale=-1.0,
                                         accum_out=den[:, i:i + 1]).then_inc(s["e"], 1)
                for kind in range(2):
                    act.wait_ge(s["os"], 2 * kind + 2)
                    nc.scalar.activation(o[:NS, TT - 1, kind * 512:(kind + 1) * 512], OS[kind][:], ACT.Copy).then_inc(s["oev"], 1)

            @block.tensor
            def _(pe):
                def scores(i):
                    kind, g = units[i]
                    if i == 0:
                        pe.wait_ge(s["qd"], 16)
                    if i >= 2:
                        pe.wait_ge(s["l"], i - 1)
                    for c in range(4):
                        nc.tensor.matmul(S[i % 2][:, PAST:], qd[:, kind, c, GB * g:GB * (g + 1), :],
                                         qkT[:, 2 * (kind * 4 + c) + 1, SEQ:], start=c == 0, stop=c == 3)
                    for bi in range(GB):
                        b = GB * g + bi
                        pe.wait_ge(kld[g], 16 * GB * (NPG + kind))
                        for c in range(4):
                            last = nc.tensor.matmul(S[i % 2][NS * bi:NS * (bi + 1), :PAST], qd[:, kind, c, b, :], kc[:, b, c, :],
                                                    start=c == 0, stop=c == 3)
                    last.then_inc(s["s_mm"], 1)

                def select(i):
                    kind, g = units[i]
                    pe.wait_ge(s["om"], i + 1)
                    nc.tensor.matmul(OS[kind][:], sel[:, g], Om[:, i % 2], start=g == 0, stop=g == 1).then_inc(s["os"], 1)

                scores(0)
                for i, (kind, g) in enumerate(units):
                    if i + 1 < 4:
                        scores(i + 1)
                    pe.wait_ge(s["e"], i + 1)
                    if i >= 2:
                        pe.wait_ge(s["et"], i - 1)
                    for b in range(NPG):
                        nc.tensor.transpose(TP[i % 2][:, b], E[:, i % 2, b * P:(b + 1) * P], ident[:])
                    nc.tensor.transpose(TP[i % 2][:NS, NPG], E[:, i % 2, PAST:], ident[:]).then_inc(s["t_mm"], 1)
                    pe.wait_ge(s["et"], i + 1)
                    if i >= 2:
                        pe.wait_ge(s["om"], i - 1)
                    nc.tensor.matmul(OP[i % 2][:], ET[:, i % 2, NPG], v[:, TT - 1, kind * 512:(kind + 1) * 512],
                                     start=True, stop=False, skip_group_check=True)
                    for bi in range(GB):
                        b = GB * g + bi
                        pe.wait_ge(vld[g], 16 * GB * (NPG + kind))
                        for j in range(NPG):
                            last = nc.tensor.matmul(OP[i % 2][NS * bi:NS * (bi + 1), :], ET[:, i % 2, j, NS * bi:NS * (bi + 1)],
                                                    vc[:, b, j], start=False, stop=j == NPG - 1, skip_group_check=True)
                    last.then_inc(s["pv"], 1)
                    if i >= 1:
                        select(i - 1)
                select(3)

        with ExitStack() as late:
            ohi = sb(late, "ohi", [P, KD, NTP], F32R)
            olo = sb(late, "olo", [P, KD, NTP], F32R)
            norm_stage("no", o, 2, A["g_out"], ohi, olo)
            with ExitStack() as st:
                def add_to_h(t, chunk, acc):
                    r = rows(t)
                    cols = bass.ds(chunk * 256, 256)
                    return nc.vector.tensor_tensor(h[:r, t, cols], h[:r, t, cols], acc[:r], ALU.add)

                on_sync, on_scalar, on_vector, on_tensor = token_rows_product(st, "po", ohi, olo, A["w_out"], 4, add_to_h)
                block = st.enter_context(nc.Block())
                block.sync(on_sync)
                block.scalar(on_scalar)
                block.vector(on_vector)
                block.tensor(on_tensor)
        attn.close()

        peer = ExitStack()
        x2hi = sb(peer, "x2hi", [P, KD, NTP], F32R)
        x2lo = sb(peer, "x2lo", [P, KD, NTP], F32R)
        norm_stage("nf", h, 1, A["g_ffn"], x2hi, x2lo)

        pick = ExitStack()
        I1 = sb(pick, "I1", [P, TT, P])
        I2 = sb(pick, "I2", [P, TT, P])
        GG = sb(pick, "GG", [P, TT, P])
        iota = sb(pick, "iota", [P, P])
        TK = TT * TOPK
        with ExitStack() as st:
            w = sb(st, "qw", [P, 2, KD, P])
            whi = sb(st, "qwhi", [P, 2, KD, P], F32R)
            wlo = sb(st, "qwlo", [P, 2, KD, P], F32R)
            qT = sb(st, "qT", [P, 2, NT])
            keys = sb(st, "keys", [P, 2, NK])
            sc = sb(st, "sc", [P, 2, TT, NK])
            sc2 = sb(st, "sc2", [P, 2, TT, NK])
            V8 = sb(st, "V8", [P, 2, TT, TOPK])
            X8 = sb(st, "X8", [P, 2, TT, TOPK], U32)
            XF = sb(st, "XF", [P, 2, TT, TOPK])
            cand = sb(st, "cand", [P, TT, TOPK, TOPK])
            cand2 = sb(st, "cand2", [P, TT, TOPK * TOPK])
            top = sb(st, "top", [P, TT, TOPK])
            pos = sb(st, "pos", [P, TT, TOPK], U32)
            ab = sb(st, "ab", [P, 2, TT, TOPK], U32)
            abf = sb(st, "abf", [P, 2, TT, TOPK])
            eq = sb(st, "eq", [P, 2, TT, TOPK, TOPK])
            pk = sb(st, "pk", [P, 2, TT, TOPK])
            sm = sb(st, "sm", [P, TT * NH])
            zp = [ps(st, f"qzp{i}", [P, 2, SEQ]) for i in range(2)]
            sp_ = [ps(st, f"qsp{i}", [P, 8, NK]) for i in range(2)]
            wld = [sem(f"q_wld{u}") for u in range(2)]
            names = ("c", "hi", "lo", "mm", "ev", "smm", "sev", "topk", "exin", "ex", "sum", "chain", "clr")
            s = {n: sem("q_" + n) for n in names}
            block = st.enter_context(nc.Block())

            @block.sync
            def _(sp):
                sp.dma_start(keys[:], A["sub_keys"]).then_inc(s["c"], 16)
                sp.dma_start(iota[:], A["iota"]).then_inc(s["c"], 16)
                with sp.Fori(0, NH) as j:
                    for u in range(2):
                        sp.wait_ge(s["lo"], 2 * j + u + 1)
                        sp.dma_start(w[:, u], A["w_query"][2 * j + u]).then_inc(wld[u], 16)

            @block.gpsimd
            def _(pool):
                pool.sem_inc(s["lo"], 2)
                with pool.Fori(0, NH) as j:
                    for u in range(2):
                        n = 2 * j + u
                        pool.wait_ge(s["hi"], n + 1)
                        nc.gpsimd.tensor_tensor(wlo[:, u], w[:, u], whi[:, u].bitcast(F32), ALU.subtract).then_inc(s["lo"], 1)

            @block.scalar
            def _(act):
                act.sem_inc(s["ev"], 2)
                act.sem_inc(s["sev"], 2)
                act.wait_ge(s["clr"], 1)
                with act.Fori(0, NH) as j:
                    for u in range(2):
                        n = 2 * j + u
                        act.wait_ge(wld[u], 16 * (j + 1))
                        act.wait_ge(s["mm"], n + 1)
                        nc.scalar.activation(whi[:, u], w[:, u], ACT.Copy).then_inc(s["hi"], 1)
                        act.wait_ge(s["mm"], n + 3)
                        act.wait_ge(s["smm"], n + 1)
                        nc.scalar.activation(qT[:, u].rearrange("p (a b) -> p a b", a=2), zp[u][:, :, :HALF],
                                             ACT.Copy).then_inc(s["ev"], 1)
                        act.wait_ge(s["smm"], n + 3)
                        act.wait_ge(s["topk"], j + 1)
                        nc.scalar.activation(sc[:, u, 0:TT - 1], sp_[u][:, 0:TT - 1], ACT.Copy)
                        nc.scalar.activation(sc[:NS, u, TT - 1], sp_[u][:NS, TT - 1], ACT.Copy).then_inc(s["sev"], 1)
                act.wait_ge(s["exin"], 1)
                nc.scalar.activation(GG[:], GG[:], ACT.Exp).then_inc(s["ex"], 1)

            @block.tensor
            def _(pe):
                pe.sem_inc(s["mm"], 2)
                pe.sem_inc(s["smm"], 2)
                pe.wait_ge(s["c"], 32)
                with pe.Fori(0, NH) as j:
                    for u in range(2):
                        n = 2 * j + u
                        pe.wait_ge(s["lo"], n + 3)
                        pe.wait_ge(s["ev"], n + 1)
                        for k in range(KD):
                            for f in range(2):
                                last = mm3(zp[u][:, f, :HALF], whi[:, u, k], wlo[:, u, k],
                                           x2hi[:, k, f * HALF:(f + 1) * HALF], x2lo[:, k, f * HALF:(f + 1) * HALF],
                                           k == 0, k == KD - 1)
                        last.then_inc(s["mm"], 1)
                        pe.wait_ge(s["ev"], n + 3)
                        pe.wait_ge(s["sev"], n + 1)
                        for t in range(TT):
                            r = rows(t)
                            last = nc.tensor.matmul(sp_[u][:r, t], qT[:, u, t * P:t * P + r], keys[:, u],
                                                    start=True, stop=True)
                        last.then_inc(s["smm"], 1)

            @block.vector
            def _(dve):
                nc.vector.memset(sc[:], 0.0).then_inc(s["clr"], 1)
                dve.sem_inc(s["topk"], 1)
                dve.wait_ge(s["c"], 32)
                LINKS = 14
                ut = [(u, t) for u in range(2) for t in range(TT)]
                with dve.Fori(0, NH) as j:
                    links = [0]

                    def link(ins):
                        links[0] += 1
                        ins.then_inc(s["chain"], 1)
                        dve.wait_ge(s["chain"], j * LINKS + links[0])
                        settle(dve)

                    for u in range(2):
                        dve.wait_ge(s["sev"], 2 * j + u + 3)
                    settle(dve)
                    for u, t in ut:
                        last = nc.vector.max(V8[:, u, t, 0:8], sc[:, u, t])
                    link(last)
                    for u, t in ut:
                        nc.vector.max_index(X8[:, u, t, 0:8], V8[:, u, t, 0:8], sc[:, u, t])
                        last = nc.vector.match_replace(sc2[:, u, t], V8[:, u, t, 0:8], sc[:, u, t], -3.0e38)
                    link(last)
                    for u, t in ut:
                        last = nc.vector.max(V8[:, u, t, 8:16], sc2[:, u, t])
                    link(last)
                    for u, t in ut:
                        last = nc.vector.max_index(X8[:, u, t, 8:16], V8[:, u, t, 8:16], sc2[:, u, t])
                    link(last)
                    nc.vector.tensor_copy(XF[:], X8[:])
                    link(nc.vector.tensor_tensor(cand[:], V8[:, 0].unsqueeze(3).broadcast_to([P, TT, TOPK, TOPK]),
                                                 V8[:, 1].unsqueeze(2).broadcast_to([P, TT, TOPK, TOPK]), ALU.add))
                    flat = [cand[:, t].rearrange("p a b -> p (a b)") for t in range(TT)]
                    for t in range(TT):
                        last = nc.vector.max(top[:, t, 0:8], flat[t])
                    link(last)
                    for t in range(TT):
                        nc.vector.max_index(pos[:, t, 0:8], top[:, t, 0:8], flat[t])
                        last = nc.vector.match_replace(cand2[:, t], top[:, t, 0:8], flat[t], -3.0e38)
                    link(last)
                    for t in range(TT):
                        last = nc.vector.max(top[:, t, 8:16], cand2[:, t])
                    link(last)
                    for t in range(TT):
                        last = nc.vector.max_index(pos[:, t, 8:16], top[:, t, 8:16], cand2[:, t])
                    link(last)
                    nc.vector.tensor_scalar(ab[:, 0], pos[:], 4, None, ALU.logical_shift_right)
                    link(nc.vector.tensor_scalar(ab[:, 1], pos[:], 15, None, ALU.bitwise_and))
                    link(nc.vector.tensor_copy(abf[:], ab[:]))
                    ranks = iota[:, 0:TOPK].unsqueeze(1).broadcast_to([P, 2 * TK, TOPK])
                    link(nc.vector.tensor_tensor(eq[:].rearrange("p u t k a -> p (u t k) a"), ranks,
                                                 abf[:].rearrange("p u t k -> p (u t k)").unsqueeze(2).broadcast_to([P, 2 * TK, TOPK]),
                                                 ALU.is_equal))
                    for u in range(2):
                        last = nc.vector.tensor_tensor(eq[:, u], eq[:, u], XF[:, u].unsqueeze(2).broadcast_to([P, TT, TOPK, TOPK]),
                                                       ALU.mult)
                    link(last)
                    link(nc.vector.tensor_reduce(pk[:], eq[:], axis=AX.X, op=ALU.add))
                    assert links[0] == LINKS, links[0]
                    nc.vector.tensor_copy(GG[:, :, bass.ds(j * TOPK, TOPK)], top[:])
                    nc.vector.tensor_copy(I1[:, :, bass.ds(j * TOPK, TOPK)], pk[:, 0])
                    nc.vector.tensor_copy(I2[:, :, bass.ds(j * TOPK, TOPK)], pk[:, 1]).then_inc(s["topk"], 1)
                heads = GG[:].rearrange("p t (h k) -> p (t h) k", k=TOPK)
                first = sb(st, "first", [P, TT * NH])
                dve.wait_ge(s["topk"], 1 + NH)
                nc.vector.tensor_copy(first[:].unsqueeze(2), heads[:, :, 0:1]).then_inc(s["sum"], 1)
                dve.wait_ge(s["sum"], 1)
                nc.vector.tensor_tensor(heads, heads, first[:].unsqueeze(2).broadcast_to([P, TT * NH, TOPK]),
                                        ALU.subtract).then_inc(s["exin"], 1)
                dve.wait_ge(s["ex"], 1)
                nc.vector.tensor_reduce(sm[:], heads, axis=AX.X, op=ALU.add).then_inc(s["sum"], 1)
                dve.wait_ge(s["sum"], 2)
                nc.vector.reciprocal(sm[:], sm[:]).then_inc(s["sum"], 1)
                dve.wait_ge(s["sum"], 3)
                nc.vector.tensor_tensor(heads, heads, sm[:].unsqueeze(2).broadcast_to([P, TT * NH, TOPK]), ALU.mult)

        with ExitStack() as st:
            slotT = sb(st, "slotT", [P, 3, NT])
            chunkT = sb(st, "chunkT", [P, 2, 3, CH])
            oh = sb(st, "oh", [P, 2, 4, P])
            og = sb(st, "og", [P, 2, 4, P])
            gst = sb(st, "gst", [P, 2, NK, CH])
            tp = [ps(st, f"gtp{i}", [P, 2, SEQ]) for i in range(3)]
            gp = [ps(st, f"ggp{i}", [P, 4, P]) for i in range(2)]
            names = ("tr", "trev", "cut", "oh", "mm", "ev", "part")
            s = {n: sem("g_" + n) for n in names}
            stored = [sem(f"g_stored{u}") for u in range(2)]
            block = st.enter_context(nc.Block())
            GR = CH // 4
            groups = [(u, r) for u in range(2) for r in range(GR)]
            N2 = 2 * GR

            @block.tensor
            def _(pe):
                for i, src in enumerate((I1, I2, GG)):
                    for t in range(TT):
                        r = rows(t)
                        last = nc.tensor.transpose(tp[i][:, t // 4, (t % 4) * P:(t % 4) * P + r], src[:r, t], ident[:r, :r])
                    last.then_inc(s["tr"], 1)
                pe.sem_inc(s["mm"], 2)
                with pe.Fori(0, NCH // 2) as j:
                    for i, (u, r) in enumerate(groups):
                        pe.wait_ge(s["oh"], j * N2 + i + 1)
                        pe.wait_ge(s["ev"], j * N2 + i + 1)
                        for k in range(4):
                            last = nc.tensor.matmul(gp[i % 2][:, k], oh[:, i % 2, k], og[:, i % 2, k], start=True, stop=True)
                        last.then_inc(s["mm"], 1)

            @block.gpsimd
            def _(pool):
                pool.wait_ge(s["trev"], 3)
                with pool.Fori(0, NCH // 2) as j:
                    for u in range(2):
                        pool.wait_ge(s["part"], 2 * j + u + 1)
                        nc.gpsimd.tensor_copy(chunkT[:, u], slotT[:, :, bass.ds((2 * j + u) * CH, CH)]).then_inc(s["cut"], 1)

            @block.vector
            def _(dve):
                dve.sem_inc(s["part"], 2)
                with dve.Fori(0, NCH // 2) as j:
                    for i, (u, r) in enumerate(groups):
                        if r == 0:
                            dve.wait_ge(s["cut"], 2 * j + u + 1)
                        dve.wait_ge(s["mm"], j * N2 + i + 1)
                        for k in range(4):
                            c = 4 * r + k
                            nc.vector.tensor_scalar(oh[:, i % 2, k], iota[:], chunkT[:, u, 1, c:c + 1], None, ALU.is_equal)
                            last = nc.vector.tensor_scalar(og[:, i % 2, k], iota[:], chunkT[:, u, 0, c:c + 1],
                                                           chunkT[:, u, 2, c:c + 1], ALU.is_equal, ALU.mult)
                        last.then_inc(s["oh"], 1)
                        if r == GR - 1:
                            dve.wait_ge(s["oh"], j * N2 + i + 1)
                            dve.sem_inc(s["part"], 1)

            @block.scalar
            def _(act):
                for i in range(3):
                    act.wait_ge(s["tr"], i + 1)
                    nc.scalar.activation(slotT[:, i, :SEQ], tp[i][:, 0], ACT.Copy)
                    nc.scalar.activation(slotT[:, i, SEQ:], tp[i][:, 1, :NS], ACT.Copy).then_inc(s["trev"], 1)
                act.sem_inc(s["ev"], 2)
                act.sem_inc(stored[0], 16)
                act.sem_inc(stored[1], 16)
                with act.Fori(0, NCH // 2) as j:
                    for i, (u, r) in enumerate(groups):
                        if r == 0:
                            act.wait_ge(stored[u], 16 * (j + 1))
                        act.wait_ge(s["mm"], j * N2 + i + 3)
                        nc.scalar.activation(gst[:, u, :, 4 * r:4 * r + 4], gp[i % 2][:].rearrange("p t i -> p i t"),
                                             ACT.Copy).then_inc(s["ev"], 1)

            @block.sync
            def _(sp):
                with sp.Fori(0, NCH // 2) as j:
                    for u in range(2):
                        sp.wait_ge(s["ev"], j * N2 + (u + 1) * GR + 2)
                        sp.dma_start(gate_dram[2 * j + u], gst[:, u]).then_inc(stored[u], 16)
                for u in range(2):
                    sp.wait_ge(stored[u], 16 * (NCH // 2 + 1))
        pick.close()

        acc = sb(peer, "acc", [P, KD, NT])
        with ExitStack() as st:
            uw = sb(st, "uw", [P, 2, KD, P])
            uhi = sb(st, "uhi", [P, 2, KD, P], F32R)
            ulo = sb(st, "ulo", [P, 2, KD, P], F32R)
            vw = sb(st, "vw", [P, 2, D])
            vhi = sb(st, "vhi", [P, GT, D], F32R)
            vlo = sb(st, "vlo", [P, GT, D], F32R)
            gt = sb(st, "gt", [P, 2, NCH, GT, CH])
            ge = sb(st, "gelu", [P, 2, NT])
            af = sb(st, "af", [P, 2, NT])
            ahi = sb(st, "ahi", [P, 2, GT, NT], F32R)
            alo = sb(st, "alo", [P, 2, GT, NT], F32R)
            hp = [ps(st, f"hp{i}", [P, 2, SEQ]) for i in range(2)]
            vp = [ps(st, f"vp{i}", [P, 2, SEQ]) for i in range(2)]
            uld = [sem(f"x_uld{u}") for u in range(2)]
            vld = [sem(f"x_vld{u}") for u in range(2)]
            gld = [sem(f"x_gld{u}") for u in range(2)]
            names = ("uhi", "ulo", "hmm", "gelu", "a", "ahi", "alo", "vhi", "vlo", "vmm", "acc", "clear")
            s = {n: sem("x_" + n) for n in names}
            block = st.enter_context(nc.Block())

            def sequence(eng, h_phase, v_phase):
                h_phase(0, 0, True, False)
                with eng.Fori(0, NG // 2 - 1) as j:
                    for u in range(2):
                        h_phase(2 * j + u + 1, (u + 1) % 2, False, False)
                        v_phase(2 * j + u, u)
                h_phase(NG - 1, 1, False, True)
                v_phase(NG - 2, 0)
                h_phase(NG, 0, False, None)
                v_phase(NG - 1, 1)

            @block.sync
            def _(sp):
                def h_phase(g, par, first, last):
                    if last is None:
                        return
                    for i in range(GT):
                        m = g * GT + i
                        sp.wait_ge(s["ulo"], m + 1)
                        sp.dma_start(uw[:, i % 2], A["u_experts"][m]).then_inc(uld[i % 2], 16)
                        if i == 0:
                            sp.wait_ge(s["a"], m + GT)
                            sp.dma_start(gt[:, par].rearrange("p c i t -> p c (i t)"),
                                         gate_dram[:, :, bass.ds(g * GT, GT), :].rearrange("c p i t -> p c (i t)")).then_inc(gld[par], 16)

                sequence(sp, h_phase, lambda g, par: None)

            @block.gpsimd
            def _(pool):
                with pool.Fori(0, NK // 2) as j:
                    for u in range(2):
                        pool.wait_ge(s["vlo"], 2 * j + u + 1)
                        pool.dma_start(vw[:, u], A["v_experts"][2 * j + u]).then_inc(vld[u], 16)

            @block.scalar
            def _(act):
                def u_split(m, slot):
                    act.wait_ge(uld[slot], (m - slot) * 8 + 16)
                    act.wait_ge(s["hmm"], m + 1)
                    nc.scalar.activation(uhi[:, slot], uw[:, slot], ACT.Copy).then_inc(s["uhi"], 1)

                def v_split(m, i):
                    act.wait_ge(vld[i % 2], (m - i % 2) * 8 + 16)
                    act.wait_ge(s["vmm"], (m - i) * (KD // GT) + KD)
                    nc.scalar.activation(vhi[:, i], vw[:, i % 2], ACT.Copy).then_inc(s["vhi"], 1)

                def h_phase(g, par, first, last):
                    for i in range(GT):
                        m = g * GT + i
                        if last is not None:
                            if not (last and i == GT - 1):
                                u_split(m + 1, (i + 1) % 2)
                            act.wait_ge(s["hmm"], m + 3)
                            act.wait_ge(s["a"], m + 1 + 2 * GT - 2)
                            nc.scalar.activation(ge[:, i % 2].rearrange("p (a b) -> p a b", a=2), hp[i % 2][:, :, :HALF],
                                                 ACT.Gelu).then_inc(s["gelu"], 1)
                            act.wait_ge(s["a"], m + 1 + 2 * GT)
                            act.wait_ge(s["vmm"], g * KD if not first else 1)
                            nc.scalar.activation(ahi[:, par, i], af[:, i % 2], ACT.Copy).then_inc(s["ahi"], 1)
                        if not first:
                            v_split(m - GT, i)

                act.sem_inc(s["gelu"], 2)
                u_split(0, 0)
                sequence(act, h_phase, lambda g, par: None)

            @block.vector
            def _(dve):
                def u_split(m, slot):
                    dve.wait_ge(s["uhi"], m + 1)
                    nc.vector.tensor_tensor(ulo[:, slot], uw[:, slot], uhi[:, slot].bitcast(F32), ALU.subtract).then_inc(s["ulo"], 1)

                def v_split(m, i):
                    dve.wait_ge(s["vhi"], m + 1)
                    nc.vector.tensor_tensor(vlo[:, i], vw[:, i % 2], vhi[:, i].bitcast(F32), ALU.subtract).then_inc(s["vlo"], 1)

                def h_phase(g, par, first, last):
                    for i in range(GT):
                        m = g * GT + i
                        if last is not None:
                            if not (last and i == GT - 1):
                                u_split(m + 1, (i + 1) % 2)
                            if i == 0:
                                dve.wait_ge(gld[par], (g - par) * 8 + 16)
                            dve.wait_ge(s["gelu"], m + 3)
                            dve.wait_ge(s["alo"], m + 1)
                            nc.vector.tensor_tensor(af[:, i % 2].rearrange("p (c t) -> p c t", c=NCH),
                                                    ge[:, i % 2].rearrange("p (c t) -> p c t", c=NCH),
                                                    gt[:, par, :, i], ALU.mult).then_inc(s["a"], 1)
                            dve.wait_ge(s["ahi"], m + 1)
                            nc.vector.tensor_tensor(alo[:, par, i], af[:, i % 2], ahi[:, par, i].bitcast(F32),
                                                    ALU.subtract).then_inc(s["alo"], 1)
                        if not first:
                            v_split(m - GT, i)

                def v_phase(g, par):
                    for k in range(KD):
                        dve.wait_ge(s["vmm"], g * KD + k + 1 + KD)
                        dst = acc[:, k].rearrange("p (a b) -> p a b", a=2)
                        nc.vector.tensor_tensor(dst, dst, vp[k % 2][:, :, :HALF], ALU.add).then_inc(s["acc"], 1)

                nc.vector.memset(acc[:], 0.0).then_inc(s["clear"], 1)
                dve.wait_ge(s["clear"], 1)
                dve.sem_inc(s["ulo"], 2)
                dve.sem_inc(s["vlo"], 2)
                dve.sem_inc(s["alo"], 2)
                dve.sem_inc(s["a"], 2 * GT)
                dve.sem_inc(s["acc"], 2)
                u_split(0, 0)
                sequence(dve, h_phase, v_phase)

            @block.tensor
            def _(pe):
                pe.sem_inc(s["hmm"], 2)
                pe.sem_inc(s["vmm"], KD)

                def h_phase(g, par, first, last):
                    if last is None:
                        return
                    for i in range(GT):
                        m = g * GT + i
                        pe.wait_ge(s["ulo"], m + 3)
                        pe.wait_ge(s["gelu"], m + 1)
                        for k in range(KD):
                            for f in range(2):
                                cols = slice(f * HALF, (f + 1) * HALF)
                                ins = mm3(hp[i % 2][:, f, :HALF], uhi[:, i % 2, k], ulo[:, i % 2, k],
                                          x2hi[:, k, cols], x2lo[:, k, cols], k == 0, k == KD - 1)
                        ins.then_inc(s["hmm"], 1)

                def v_phase(g, par):
                    pe.wait_ge(s["vlo"], g * GT + GT + 2)
                    pe.wait_ge(s["alo"], g * GT + GT + 2)
                    for k in range(KD):
                        pe.wait_ge(s["acc"], g * KD + k + 1)
                        for i in range(GT):
                            for f in range(2):
                                cols = slice(f * HALF, (f + 1) * HALF)
                                ins = mm3(vp[k % 2][:, f, :HALF], vhi[:, i, k * P:(k + 1) * P], vlo[:, i, k * P:(k + 1) * P],
                                          ahi[:, par, i, cols], alo[:, par, i, cols], i == 0, i == GT - 1)
                        ins.then_inc(s["vmm"], 1)

                sequence(pe, h_phase, v_phase)

        with ExitStack() as st:
            y = sb(st, "y", [P, TT, D])
            sq = sb(st, "fsq", [P, D])
            gf = sb(st, "gf", [P, D])
            ssq = sb(st, "fssq", [P, TT])
            root = sb(st, "froot", [P, TT])
            tp = [ps(st, f"ftp{i}", [P, KD, P]) for i in range(2)]
            names = ("ld", "tr", "sum", "sq", "ms", "root", "inv", "scaled", "y", "out")
            s = {n: sem("n_" + n) for n in names}
            block = st.enter_context(nc.Block())

            @block.tensor
            def _(pe):
                for t in range(TT):
                    r = rows(t)
                    if t >= 2:
                        pe.wait_ge(s["sum"], t - 1)
                    for k in range(KD):
                        last = nc.tensor.transpose(tp[t % 2][:r, k], acc[:, k, t * P:t * P + r], ident[:])
                    last.then_inc(s["tr"], 1)

            @block.vector
            def _(dve):
                nc.vector.memset(ssq[:], 1.0).then_inc(s["ms"], 1)
                for t in range(TT):
                    r = rows(t)
                    dve.wait_ge(s["tr"], t + 1)
                    nc.vector.tensor_tensor(h[:r, t], h[:r, t], tp[t % 2][:r].rearrange("p k n -> p (k n)"), ALU.add).then_inc(s["sum"], 1)
                dve.wait_ge(s["sq"], TT)
                nc.vector.tensor_scalar(ssq[:], ssq[:], 1.0 / D, EPS, ALU.mult, ALU.add).then_inc(s["ms"], 1)
                dve.wait_ge(s["root"], 1)
                nc.vector.reciprocal(ssq[:], root[:]).then_inc(s["inv"], 1)
                dve.wait_ge(s["ld"], 16)
                for t in range(TT):
                    r = rows(t)
                    dve.wait_ge(s["scaled"], t + 1)
                    nc.vector.tensor_tensor(y[:r, t], y[:r, t], gf[:r], ALU.mult).then_inc(s["y"], 1)

            @block.scalar
            def _(act):
                act.wait_ge(s["ms"], 1)
                for t in range(TT):
                    r = rows(t)
                    act.wait_ge(s["sum"], t + 1)
                    if t:
                        act.wait_ge(s["sq"], t)
                    nc.scalar.activation(sq[:r], h[:r, t], ACT.Square, accum_out=ssq[:r, t:t + 1]).then_inc(s["sq"], 1)
                act.wait_ge(s["ms"], 2)
                nc.scalar.activation(root[:], ssq[:], ACT.Sqrt).then_inc(s["root"], 1)
                act.wait_ge(s["inv"], 1)
                for t in range(TT):
                    r = rows(t)
                    nc.scalar.activation(y[:r, t], h[:r, t], ACT.Copy, scale=ssq[:r, t:t + 1]).then_inc(s["scaled"], 1)

            @block.sync
            def _(sp):
                sp.dma_start(gf[:], A["g_final"].broadcast_to([P, D])).then_inc(s["ld"], 16)
                sp.wait_ge(s["y"], TT - 1)
                sp.dma_start(O["y_prompt"].rearrange("(t p) d -> p t d", p=P), y[:, 0:TT - 1]).then_inc(s["out"], 16)
                sp.wait_ge(s["y"], TT)
                sp.dma_start(O["y_sample"], y[:NS, TT - 1]).then_inc(s["out"], 16)
                sp.wait_ge(s["out"], 32)
        peer.close()
        persistent.close()


def bucket(dist):
    exact = NBK // 2
    d = np.maximum(dist, 1).astype(np.float32)
    large = exact + (np.log(d / exact) / math.log(2048 / exact) * (NBK - exact)).astype(np.int32)
    return np.where(dist < exact, dist, np.minimum(large, NBK - 1))


def bias_row_constants():
    dist = SEQ - 1 - np.arange(DIST)
    count = sum(((dist >= 0) & (dist <= window) & (dist % dil == 0)).astype(np.float32)
                for window, dil in ((128, 1), (512, 4), (2048, 16)))
    out = np.zeros((NBK + 2, DIST), np.float32)
    back = dist >= 0
    out[bucket(np.maximum(dist, 0))[back], np.arange(DIST)[back]] = 1.0
    out[NBK] = np.where(count > 0, np.log(np.maximum(count, 1)), NEG)
    out[NBK + 1] = np.where(back, 0.0, NEG)
    kind = np.zeros((2, 2 * NH), np.float32)
    kind[0, NH:] = 1.0
    kind[1, :NH] = 1.0
    return out, kind


def sample_row_constants():
    r = np.arange(P)
    mask = (r[:, None] // DEC_S % NH == np.arange(NH)).astype(np.float32)
    sel = np.zeros((P, 2, NS), np.float32)
    for g in range(2):
        sel[r, g, g * 4 * DEC_S + r // NS * DEC_S + r % DEC_S] = 1.0
    return mask, sel


def kernel(**inputs):
    import concourse.bacc as bacc
    from concourse.bass_utils import run_bass_kernel_spmd

    x = {k: np.asarray(a) for k, a in inputs.items()}

    def columns(w, width):
        return np.ascontiguousarray(w.reshape(KD, P, -1, width).transpose(2, 1, 0, 3))

    w_in = x["w_in"][0]
    F = NH * HD
    qf, kf, vf, qd, kd, vd = (w_in[:, i * F:(i + 1) * F] for i in range(6))
    qk = np.stack([columns(a, P) for a in (qf, kf, qd, kd)]).reshape(2, 2, 4, P, KD, P)
    qk = qk.transpose(0, 2, 1, 3, 4, 5).reshape(4 * 4, P, KD, P)
    pool = x["cache_k_fox"].shape[1]
    onehot, kind = bias_row_constants()
    head_mask, row_select = sample_row_constants()
    gamma = lambda g: g.reshape(KD, P).T
    arrays = {
        "x_prompt": x["x_prompt"][0], "x_sample": x["x_sample"].reshape(NS, D),
        "w_qk": qk, "w_v": columns(np.concatenate([vf, vd], 1), 256),
        "w_f": w_in[:, 6 * F:].reshape(KD, P, NH).transpose(1, 0, 2), "b_f": x["b_fgate"].reshape(NH, 1),
        "g_attn": gamma(x["g_attn"][0]), "g_ffn": gamma(x["g_ffn"][0]),
        "g_out": gamma(np.concatenate([x["g_out_fox"][0], x["g_out_dil"][0]])),
        "g_final": x["g_final"].reshape(1, D),
        "w_out": columns(x["w_out"][0], 256), "w_query": columns(x["w_query"][0], P),
        "sub_keys": x["sub_keys"][0].transpose(2, 0, 1),
        "rel_bias": x["rel_bias"],
        "k_pages": x["cache_k_fox"][0].reshape(pool, PAGE, 4, P).transpose(0, 3, 2, 1),
        "v_pages": x["cache_v_fox"][0].reshape(pool, PAGE, F),
        "logf_pages": x["cache_logf_fox"][0].transpose(0, 2, 1),
        "k_win": x["cache_k_win"][0].reshape(DEC_B, PAST, 4, P).transpose(0, 3, 2, 1),
        "v_win": x["cache_v_win"][0].reshape(DEC_B, PAST, F),
        "page_table": x["page_table"].reshape(1, -1).astype(np.int32),
        "u_experts": x["u_experts"][0].reshape(NK, P, KD, P).transpose(0, 3, 2, 1),
        "v_experts": x["v_experts"][0].reshape(NK, P, D),
        "ident": np.eye(P, dtype=np.float32), "bucket_onehot": onehot, "row_kind": kind,
        "head_mask": head_mask, "row_select": row_select,
        "iota": np.tile(np.arange(P, dtype=np.float32), (P, 1)),
    }
    arrays = {"in_" + k: np.ascontiguousarray(a) for k, a in arrays.items()}
    outs = {"y_prompt": (SEQ, D), "y_sample": (NS, D), "lfp": (SEQ, NH), "lfs": (NS, NH)}
    for name in ("kf", "vf", "kw", "vw"):
        outs[name + "p"] = (SEQ, F)
        outs[name + "s"] = (NS, F)

    nc = bacc.Bacc("TRN2", target_bir_lowering=False, num_devices=1)
    A = {k[3:]: nc.dram_tensor(k, a.shape, mybir.dt.from_np(a.dtype), kind="ExternalInput").ap() for k, a in arrays.items()}
    O = {k: nc.dram_tensor("out_" + k, shape, F32, kind="ExternalOutput").ap() for k, shape in outs.items()}
    build(nc, A, O)
    r = run_bass_kernel_spmd(nc, [arrays], core_ids=[0]).results[0]
    got = {k: r["out_" + k] for k in outs}
    prompt = lambda a: a.reshape(1, 1, SEQ, NH, HD)
    sample = lambda a: a.reshape(1, DEC_B, DEC_S, NH, HD)
    return (got["y_prompt"].reshape(1, SEQ, D), got["y_sample"].reshape(DEC_B, DEC_S, D),
            prompt(got["kfp"]), prompt(got["vfp"]), got["lfp"].reshape(1, 1, SEQ, NH),
            sample(got["kfs"]), sample(got["vfs"]), got["lfs"].reshape(1, DEC_B, DEC_S, NH),
            prompt(got["kwp"]), prompt(got["vwp"]), sample(got["kws"]), sample(got["vws"]))
```

```python
import math

import numpy as np
import concourse.bass as bass
from concourse import mybir
from contextlib import ExitStack

F32 = mybir.dt.float32
F32R = mybir.dt.float32r
U32 = mybir.dt.uint32
ACT = mybir.ActivationFunctionType
ALU = mybir.AluOpType
AX = mybir.AxisListType

P = 128
D = 1024
KD = D // P
SEQ, DEC_B, DEC_S, PAST = 512, 8, 4, 256
PAGE = 128
NS = DEC_B * DEC_S
NT = SEQ + NS
TT = SEQ // P + 1
NTP = TT * P
HALF = NT // 2
HD, NH = 64, 8
PAIRS = NH
NBK = 32
NEG = -1.0e30
EPS = 1e-6
NK = 128
TOPK = 16
DIST = SEQ + P
SCALE8 = HD ** 0.5
CH = 34
NCH = NT // CH
GT = 4
NG = NK // GT


def rows(t):
    return P if t < TT - 1 else NS


def build(nc, A, O):
    ctx = ExitStack()
    persistent = ExitStack()

    def sem(name):
        return ctx.enter_context(nc.semaphore(name))

    def sb(stack, name, shape, dt=F32):
        return stack.enter_context(nc.sbuf_tensor(name, shape, dt))

    def ps(stack, name, shape):
        return stack.enter_context(nc.psum_tensor(name, shape, F32))

    bias_dram = nc.dram_tensor("bias_rows", (2 * NH, DIST), F32, kind="Internal").ap()
    tile_dram = nc.dram_tensor("bias_tiles", (2 * NH, P, SEQ), F32, kind="Internal").ap()
    cum_dram = nc.dram_tensor("cum_rows", (2 * NH, SEQ), F32, kind="Internal").ap()
    logf_dram = nc.dram_tensor("logf_rows", (NH, NT), F32, kind="Internal").ap()
    gate_dram = nc.dram_tensor("gate_matrix", (NCH, P, NK, CH), F32, kind="Internal").ap()
    gelu_dram = nc.dram_tensor("hidden_values", (NK, P, NT), F32, kind="Internal").ap()

    with ctx:
        ident = sb(ctx, "ident", [P, P])
        h = sb(persistent, "h", [P, TT, D])
        tiles_done = sem("tiles_done")
        passed = sem("passed")

        def settle(eng):
            eng.sem_inc(passed, 1)


        NORM_SEMS = ("loaded", "cleared", "squared", "meaned", "rooted", "inverted", "scaled", "turned", "gained",
                     "split_hi", "split_lo", "chain")
        norm_sems = {n: sem("norm_" + n) for n in NORM_SEMS}
        norm_ends = {n: 0 for n in NORM_SEMS}

        def norm_stage(tag, src, parts, gamma_dram, hi, lo, first_loads=None):
            W = D // parts
            with ExitStack() as st:
                gamma = sb(st, tag + "_gamma", [P, KD])
                ssq = sb(st, tag + "_ssq", [P, TT, parts])
                rstd = sb(st, tag + "_rstd", [P, TT, parts])
                rsq_tmp = sb(st, tag + "_rsq", [P, TT, parts])
                sq = sb(st, tag + "_sq", [P, D])
                xs = sb(st, tag + "_xs", [P, 2, D])
                full = sb(st, tag + "_full", [P, 2, KD, P])
                tp = [ps(st, f"{tag}_tp{i}", [P, KD, P]) for i in range(2)]
                loaded, cleared, squared, meaned, rooted, inverted, scaled, turned, gained, split_hi, split_lo, chain = (
                    norm_sems[n] for n in NORM_SEMS)
                base = dict(norm_ends)
                n_loads = 0 if first_loads is None else first_loads[0]
                block = st.enter_context(nc.Block())

                @block.sync
                def _(sp):
                    sp.dma_start(gamma[:], gamma_dram).then_inc(loaded, 16)
                    if first_loads is not None:
                        first_loads[1](sp, loaded)

                @block.gpsimd
                def _(pool):
                    if hi.shape[2] > NT:
                        nc.gpsimd.memset(hi[:, :, NT:].bitcast(F32), 0.0).then_inc(cleared, 1)
                        nc.gpsimd.memset(lo[:, :, NT:].bitcast(F32), 0.0).then_inc(cleared, 1)

                def split(act, t):
                    r = rows(t)
                    act.wait_ge(gained, base["gained"] + t + 1)
                    nc.scalar.activation(hi[:, :, t * P:t * P + r], full[:, t % 2, :, :r], ACT.Copy).then_inc(split_hi, 1)

                @block.scalar
                def _(act):
                    act.wait_ge(loaded, base["loaded"] + 16 * (1 + n_loads))
                    act.wait_ge(meaned, base["meaned"] + 1)
                    for t in range(TT):
                        r = rows(t)
                        for g in range(parts):
                            if t or g:
                                act.wait_ge(squared, base["squared"] + t * parts + g)
                            nc.scalar.activation(sq[:r, g * W:(g + 1) * W], src[:r, t, g * W:(g + 1) * W], ACT.Square,
                                                 accum_out=ssq[:r, t, g:g + 1]).then_inc(squared, 1)
                    act.wait_ge(meaned, base["meaned"] + 2)
                    nc.scalar.activation(rstd[:], ssq[:], ACT.Sqrt).then_inc(rooted, 1)
                    act.wait_ge(inverted, base["inverted"] + 1)
                    for t in range(TT):
                        r = rows(t)
                        if t >= 2:
                            act.wait_ge(turned, base["turned"] + t - 1)
                        for g in range(parts):
                            nc.scalar.activation(xs[:r, t % 2, g * W:(g + 1) * W], src[:r, t, g * W:(g + 1) * W],
                                                 ACT.Copy, scale=ssq[:r, t, g:g + 1]).then_inc(scaled, 1)
                        if t >= 1:
                            split(act, t - 1)
                    split(act, TT - 1)

                @block.tensor
                def _(pe):
                    for t in range(TT):
                        r = rows(t)
                        pe.wait_ge(scaled, base["scaled"] + parts * (t + 1))
                        if t >= 2:
                            pe.wait_ge(gained, base["gained"] + t - 1)
                        for k in range(KD):
                            last = nc.tensor.transpose(tp[t % 2][:, k, :r], xs[:r, t % 2, k * P:(k + 1) * P], ident[:r, :r])
                        last.then_inc(turned, 1)

                @block.vector
                def _(dve):
                    nc.vector.memset(ssq[:], 1.0).then_inc(meaned, 1)
                    dve.wait_ge(squared, base["squared"] + TT * parts)
                    nc.vector.tensor_scalar(ssq[:], ssq[:], 1.0 / W, EPS, ALU.mult, ALU.add).then_inc(meaned, 1)
                    dve.wait_ge(rooted, base["rooted"] + 1)
                    rsqrt_refined(dve, ssq, rstd, rsq_tmp, chain, base["chain"]).then_inc(inverted, 1)
                    for t in range(TT):
                        r = rows(t)
                        dve.wait_ge(turned, base["turned"] + t + 1)
                        if t >= 2:
                            dve.wait_ge(split_hi, base["split_hi"] + t - 1)
                            dve.wait_ge(split_lo, base["split_lo"] + t - 1)
                        nc.vector.tensor_tensor(full[:, t % 2, :, :r], tp[t % 2][:, :, :r],
                                                gamma[:].unsqueeze(2).broadcast_to([P, KD, r]), ALU.mult).then_inc(gained, 1)
                        dve.wait_ge(split_hi, base["split_hi"] + t + 1)
                        nc.vector.tensor_tensor(lo[:, :, t * P:t * P + r], full[:, t % 2, :, :r],
                                                hi[:, :, t * P:t * P + r].bitcast(F32), ALU.subtract).then_inc(split_lo, 1)
                for n, total in zip(NORM_SEMS, (16 * (1 + n_loads), 2 * (hi.shape[2] > NT), TT * parts, 2, 1, 1, TT * parts,
                                                TT, TT, TT, TT, 4)):
                    norm_ends[n] += total

        def rsqrt_refined(dve, x, root, tmp, chain, start=0):
            count = [start]

            def link(ins):
                count[0] += 1
                ins.then_inc(chain, 1)
                dve.wait_ge(chain, count[0])

            link(nc.vector.reciprocal(root[:], root[:]))
            link(nc.vector.tensor_tensor(tmp[:], root[:], root[:], ALU.mult))
            link(nc.vector.tensor_tensor(tmp[:], tmp[:], x[:], ALU.mult))
            link(nc.vector.tensor_scalar(tmp[:], tmp[:], -0.5, 1.5, ALU.mult, ALU.add))
            return nc.vector.tensor_tensor(x[:], root[:], tmp[:], ALU.mult)

        def mm3(out, a_hi, a_lo, b_hi, b_lo, first, last):
            nc.tensor.matmul(out, a_hi, b_hi, start=first, stop=False)
            nc.tensor.matmul(out, a_hi, b_lo, start=False, stop=False)
            return nc.tensor.matmul(out, a_lo, b_hi, start=False, stop=last)

        def token_rows_product(st, tag, xhi, xlo, w, wld, w_dram, w_tiles, evacuate):
            CW = 256
            whi = sb(st, tag + "_whi", [P, 2, KD, CW], F32R)
            wlo = sb(st, tag + "_wlo", [P, 2, KD, CW], F32R)
            acc = [ps(st, f"{tag}_acc{i}", [P, CW]) for i in range(2)]
            hi_done, lo_done, mm_done, out_done = (sem(f"{tag}_{n}") for n in ("hi_done", "lo_done", "mm_done", "out_done"))

            def on_sync(sp):
                for chunk in range(2, w_tiles):
                    sp.wait_ge(lo_done, chunk - 1)
                    sp.dma_start(w[:, chunk % 2], w_dram[chunk]).then_inc(wld[chunk % 2], 16)

            def on_scalar(act, chunks=range(w_tiles)):
                for chunk in chunks:
                    act.wait_ge(wld[chunk % 2], 16 * (chunk // 2 + 1))
                    if chunk >= 2:
                        act.wait_ge(mm_done, (chunk - 1) * TT)
                    nc.scalar.activation(whi[:, chunk % 2], w[:, chunk % 2], ACT.Copy).then_inc(hi_done, 1)

            def split_lo(dve, chunk):
                dve.wait_ge(hi_done, chunk + 1)
                nc.vector.tensor_tensor(wlo[:, chunk % 2], w[:, chunk % 2], whi[:, chunk % 2].bitcast(F32),
                                        ALU.subtract).then_inc(lo_done, 1)

            def first_on_vector(dve):
                dve.sem_inc(out_done, 2)
                split_lo(dve, 0)
                split_lo(dve, 1)

            def on_vector(dve):
                for chunk in range(w_tiles):
                    for t in range(TT):
                        if t == 2 and 1 <= chunk < w_tiles - 1:
                            split_lo(dve, chunk + 1)
                        dve.wait_ge(mm_done, chunk * TT + t + 1)
                        evacuate(t, chunk, acc[(chunk * TT + t) % 2]).then_inc(out_done, 1)

            def on_tensor(pe):
                with pe.Fori(0, w_tiles // 2) as j:
                    for u in range(2):
                        pe.wait_ge(lo_done, 2 * j + u + 1)
                        for t in range(TT):
                            pe.wait_ge(out_done, (2 * j + u) * TT + t + 1)
                            for k in range(KD):
                                last = mm3(acc[(u * TT + t) % 2][:], xhi[:, k, t * P:(t + 1) * P], xlo[:, k, t * P:(t + 1) * P],
                                           whi[:, u, k], wlo[:, u, k], k == 0, k == KD - 1)
                            last.then_inc(mm_done, 1)

            return on_sync, on_scalar, first_on_vector, on_vector, on_tensor

        with ExitStack() as st:
            onehot = sb(st, "onehot", [NBK + 2, DIST])
            relw = sb(st, "relw", [NBK + 2, 2 * NH])
            brow = sb(st, "brow", [2 * NH, DIST])
            zrow = sb(st, "zrow", [NH, SEQ])
            bp = ps(st, "bp", [2 * NH, DIST])
            t_ld, t_clr, t_mm, t_ev, t_out = (sem("t_" + n) for n in ("ld", "clr", "mm", "ev", "out"))
            block = st.enter_context(nc.Block())

            @block.sync
            def _(sp):
                sp.dma_start(ident[:], A["ident"]).then_inc(t_ld, 16)
                sp.dma_start(onehot[:], A["bucket_onehot"]).then_inc(t_ld, 16)
                sp.wait_ge(t_clr, 1)
                sp.dma_start(relw[:NBK, NH:], A["rel_bias"]).then_inc(t_ld, 16)
                sp.dma_start(relw[NBK:, :], A["row_kind"]).then_inc(t_ld, 16)
                sp.wait_ge(t_ev, 2)
                sp.dma_start(bias_dram, brow[:]).then_inc(t_out, 16)
                sp.wait_ge(t_clr, 2)
                sp.dma_start(cum_dram[NH:], zrow[:]).then_inc(t_out, 16)
                sp.wait_ge(t_out, 32)
                diagonals = bass.AP(bias_dram.tensor, P - 1, [[DIST, 2 * NH], [-1, P], [1, SEQ]])
                sp.dma_start(tile_dram, diagonals).then_inc(tiles_done, 16)

            @block.vector
            def _(dve):
                nc.vector.memset(relw[:], 0.0).then_inc(t_clr, 1)
                nc.vector.memset(zrow[:], 0.0).then_inc(t_clr, 1)
                dve.wait_ge(t_mm, 2)
                nc.vector.tensor_scalar(brow[:, :SEQ], bp[:, :SEQ], SCALE8, None, ALU.mult).then_inc(t_ev, 1)
                nc.vector.tensor_scalar(brow[:, SEQ:], bp[:, SEQ:], SCALE8, None, ALU.mult).then_inc(t_ev, 1)

            @block.tensor
            def _(pe):
                pe.wait_ge(t_ld, 64)
                nc.tensor.matmul(bp[:, :SEQ], relw[:], onehot[:, :SEQ], start=True, stop=True).then_inc(t_mm, 1)
                nc.tensor.matmul(bp[:, SEQ:], relw[:], onehot[:, SEQ:], start=True, stop=True).then_inc(t_mm, 1)

        attn = ExitStack()
        qkT = sb(attn, "qkT", [P, 2 * PAIRS, NT])
        v = sb(attn, "v", [P, TT, D])

        def load_x(sp, loaded):
            sp.dma_start(h[:, 0:TT - 1, :], A["x_prompt"].rearrange("(t p) d -> p t d", p=P)).then_inc(loaded, 16)
            sp.dma_start(h[:NS, TT - 1, :], A["x_sample"]).then_inc(loaded, 16)

        proj = ExitStack()
        xhi = sb(proj, "xhi", [P, KD, NTP], F32R)
        xlo = sb(proj, "xlo", [P, KD, NTP], F32R)
        norm_stage("na", h, 1, A["g_attn"], xhi, xlo, (2, load_x))

        w_early = sb(proj, "pv_w", [P, 2, KD, 256])
        w_loaded = [sem(f"pv_wld{u}") for u in range(2)]
        with ExitStack() as st:
            w = sb(st, "pw", [P, 2, KD, P])
            whi = sb(st, "pwhi", [P, 2, KD, P], F32R)
            wlo = sb(st, "pwlo", [P, 2, KD, P], F32R)
            kz = sb(st, "kz", [P, NT])
            kn = sb(st, "kn", [P, TT, P])
            zp = [ps(st, f"zp{i}", [P, 2, SEQ]) for i in range(2)]
            kp = ps(st, "kp", [P, 8, P])
            wld = [sem(f"p_wld{u}") for u in range(2)]
            hi_done, lo_done, mm_done, ev_done, kt_done, kn_done, k_out = (
                sem("p_" + n) for n in ("hi_done", "lo_done", "mm_done", "ev_done", "kt_done", "kn_done", "k_out"))
            kcopied = sem("p_kcopied")
            kn_free = sem("p_kn_free")
            block = st.enter_context(nc.Block())
            k_outs = ((O["kfp"], O["kfs"]), (O["kwp"], O["kws"]))

            @block.sync
            def _(sp):
                for kind in range(2):
                    with sp.Fori(0, NH // 2) as j:
                        for u in range(2):
                            n = kind * NH + 2 * j + u
                            sp.wait_ge(lo_done, n + 1)
                            sp.dma_start(w[:, u], A["w_qk"][n]).then_inc(wld[u], 16)
                for u in range(2):
                    sp.dma_start(w_early[:, u], A["w_v"][u]).then_inc(w_loaded[u], 16)

            @block.scalar
            def _(act):
                act.sem_inc(ev_done, 2)

                def split(m, u):
                    act.wait_ge(wld[u], 16 * m + 16)
                    act.wait_ge(mm_done, 2 * m + u + 1)
                    nc.scalar.activation(whi[:, u], w[:, u], ACT.Copy).then_inc(hi_done, 1)

                def turn(m, last):
                    split(m, 1)
                    act.wait_ge(mm_done, 2 * m + 3)
                    nc.scalar.activation(qkT[:, 2 * m, :].rearrange("p (a b) -> p a b", a=2),
                                         zp[0][:, :, :HALF], ACT.Copy).then_inc(ev_done, 1)
                    if not last:
                        split(m + 1, 0)
                    act.wait_ge(mm_done, 2 * m + 4)
                    act.wait_ge(kt_done, m + 1)
                    act.wait_ge(kcopied, m + 1)
                    nc.scalar.activation(kz[:].rearrange("p (a b) -> p a b", a=2),
                                         zp[1][:, :, :HALF], ACT.Copy).then_inc(ev_done, 1)

                split(0, 0)
                with act.Fori(0, NH - 1) as m:
                    turn(m, False)
                turn(NH - 1, True)

            @block.vector
            def _(dve):
                dve.sem_inc(lo_done, 2)
                dve.sem_inc(kn_done, 1)
                dve.sem_inc(kcopied, 1)

                def split(m, u):
                    dve.wait_ge(hi_done, 2 * m + u + 1)
                    nc.vector.tensor_tensor(wlo[:, u], w[:, u], whi[:, u].bitcast(F32), ALU.subtract).then_inc(lo_done, 1)

                def turn(m, last):
                    split(m, 1)
                    if not last:
                        split(m + 1, 0)
                    dve.wait_ge(ev_done, 2 * m + 4)
                    nc.vector.tensor_copy(qkT[:, 2 * m + 1, :], kz[:]).then_inc(kcopied, 1)
                    dve.wait_ge(kt_done, m + 2)
                    dve.wait_ge(kn_free, m + 1)
                    nc.vector.tensor_copy(kn[:, 0:TT - 1], kp[:, 0:TT - 1])
                    nc.vector.tensor_copy(kn[:NS, TT - 1], kp[:NS, TT - 1]).then_inc(kn_done, 1)

                split(0, 0)
                with dve.Fori(0, NH - 1) as m:
                    turn(m, False)
                turn(NH - 1, True)

            @block.tensor
            def _(pe):
                pe.sem_inc(mm_done, 2)
                pe.sem_inc(kt_done, 1)

                def product(m, u):
                    pe.wait_ge(lo_done, 2 * m + u + 3)
                    pe.wait_ge(ev_done, 2 * m + u + 1)
                    for k in range(KD):
                        for f in range(2):
                            last = mm3(zp[u][:, f, :HALF], whi[:, u, k], wlo[:, u, k],
                                       xhi[:, k, f * HALF:(f + 1) * HALF], xlo[:, k, f * HALF:(f + 1) * HALF],
                                       k == 0, k == KD - 1)
                    last.then_inc(mm_done, 1)

                def turn_k(m):
                    pe.wait_ge(ev_done, 2 * m + 4)
                    pe.wait_ge(kn_done, m + 1)
                    for t in range(TT):
                        r = rows(t)
                        last = nc.tensor.transpose(kp[:r, t, :], kz[:, t * P:t * P + r], ident[:])
                    last.then_inc(kt_done, 1)

                product(0, 0)
                with pe.Fori(0, NH - 1) as m:
                    product(m, 1)
                    product(m + 1, 0)
                    turn_k(m)
                product(NH - 1, 1)
                turn_k(NH - 1)

            @block.gpsimd
            def _(pool):
                pool.sem_inc(kn_free, 1)
                for kind in range(2):
                    prompt_out, sample_out = k_outs[kind]
                    with pool.Fori(0, NH // 2) as j:
                        m = kind * (NH // 2) + j
                        pool.wait_ge(kn_done, m + 2)
                        pool.dma_start(prompt_out.rearrange("(t p) (c n) -> c p t n", p=P, n=P)[j], kn[:, 0:TT - 1]).then_inc(k_out, 16)
                        pool.dma_start(sample_out.rearrange("t (c n) -> c t n", n=P)[j], kn[:NS, TT - 1]).then_inc(k_out, 16)
                        pool.wait_ge(k_out, 32 * m + 32)
                        pool.sem_inc(kn_free, 1)
                pool.wait_ge(k_out, 32 * NH)

        with ExitStack() as st:
            def keep_v(t, chunk, acc):
                return nc.vector.tensor_copy(v[:, t, bass.ds(chunk * 256, 256)], acc[:])

            on_sync, on_scalar, first_on_vector, on_vector, on_tensor = token_rows_product(st, "pv", xhi, xlo, w_early, w_loaded, A["w_v"], 4, keep_v)
            wf = sb(st, "wf", [P, KD, NH])
            bf = sb(st, "bf", [NH, 1])
            gz, ga, ge, gu, gl, gd, gw = (sb(st, "g" + n, [NH, NT]) for n in ("z", "a", "e", "u", "l", "d", "w"))
            logf = sb(st, "logf", [NH, NT])
            cum = sb(st, "cum", [NH, SEQ])
            lf = sb(st, "lf", [P, TT, NH])
            zf = ps(st, "zf", [NH, 2, SEQ])
            lp = ps(st, "lp", [P, TT, NH])
            v_out = sem("v_out")
            f_ld, f_mm, f_act, f_dve, f_tr, f_out = (sem("f_" + n) for n in ("ld", "mm", "act", "dve", "tr", "out"))
            block = st.enter_context(nc.Block())

            @block.sync
            def _(sp):
                sp.dma_start(wf[:], A["w_f"]).then_inc(f_ld, 16)
                sp.dma_start(bf[:], A["b_f"]).then_inc(f_ld, 16)
                sp.wait_ge(f_dve, 10)
                sp.dma_start(logf_dram, logf[:]).then_inc(f_out, 16)
                sp.dma_start(cum_dram[:NH], cum[:]).then_inc(f_out, 16)
                on_sync(sp)
                sp.wait_ge(f_dve, 11)
                sp.dma_start(O["lfp"].rearrange("(t p) h -> p t h", p=P), lf[:, 0:TT - 1]).then_inc(f_out, 16)
                sp.dma_start(O["lfs"], lf[:NS, TT - 1]).then_inc(f_out, 16)
                for kind, (prompt_out, sample_out) in enumerate(((O["vfp"], O["vfs"]), (O["vwp"], O["vws"]))):
                    sp.dma_start(prompt_out.rearrange("(t p) n -> p t n", p=P),
                                 v[:, 0:TT - 1, kind * 512:(kind + 1) * 512]).then_inc(v_out, 16)
                    sp.dma_start(sample_out, v[:NS, TT - 1, kind * 512:(kind + 1) * 512]).then_inc(v_out, 16)
                sp.wait_ge(f_out, 64)

            @block.scalar
            def _(act):
                on_scalar(act, range(2))
                act.wait_ge(f_ld, 32)
                act.wait_ge(f_mm, 1)
                nc.scalar.activation(gz[:].rearrange("p (a b) -> p a b", a=2), zf[:, :, :HALF], ACT.Identity,
                                     bias=bf[:]).then_inc(f_act, 1)
                act.wait_ge(f_act, 1)
                nc.scalar.activation(ga[:], gz[:], ACT.Abs).then_inc(f_act, 1)
                act.wait_ge(f_act, 2)
                nc.scalar.activation(ge[:], ga[:], ACT.Exp, scale=-1.0).then_inc(f_act, 1)
                act.wait_ge(f_dve, 1)
                nc.scalar.activation(gl[:], gu[:], ACT.Ln).then_inc(f_act, 1)
                on_scalar(act, range(2, 4))

            @block.vector
            def _(dve):
                first_on_vector(dve)
                count = [0]

                def step(ins):
                    count[0] += 1
                    ins.then_inc(f_dve, 1)
                    dve.wait_ge(f_dve, count[0])

                dve.wait_ge(f_act, 3)
                step(nc.vector.tensor_scalar(gu[:], ge[:], 1.0, None, ALU.add))
                step(nc.vector.tensor_scalar(gd[:], gu[:], -1.0, None, ALU.add))
                step(nc.vector.tensor_scalar(gw[:], gd[:], 0.0, None, ALU.is_equal))
                step(nc.vector.tensor_tensor(gd[:], gd[:], gw[:], ALU.add))
                step(nc.vector.reciprocal(gd[:], gd[:]))
                dve.wait_ge(f_act, 4)
                step(nc.vector.tensor_tensor(gw[:], gl[:], gw[:], ALU.add))
                step(nc.vector.tensor_tensor(gd[:], gd[:], gw[:], ALU.mult))
                step(nc.vector.tensor_tensor(gd[:], gd[:], ge[:], ALU.mult))
                step(nc.vector.scalar_tensor_tensor(logf[:], gz[:], 0.0, gd[:], ALU.min, ALU.subtract))
                nc.vector.memset(ga[:], 1.0).then_inc(f_tr, 1)
                dve.wait_ge(f_tr, 1)
                nc.vector.tensor_tensor_scan(cum[:], ga[:, :SEQ], logf[:, :SEQ], 0.0, ALU.mult, ALU.add).then_inc(f_tr, 1)
                dve.wait_ge(f_tr, 2)
                step(nc.vector.tensor_scalar(cum[:], cum[:], -SCALE8, None, ALU.mult))
                on_vector(dve)
                dve.wait_ge(f_mm, 2)
                nc.vector.tensor_copy(lf[:, 0:TT - 1], lp[:, 0:TT - 1])
                step(nc.vector.tensor_copy(lf[:NS, TT - 1], lp[:NS, TT - 1]))

            @block.tensor
            def _(pe):
                pe.wait_ge(f_ld, 32)
                for f in range(2):
                    cols = slice(f * HALF, (f + 1) * HALF)
                    for k in range(KD):
                        nc.tensor.matmul(zf[:, f, :HALF], wf[:, k], xhi[:, k, cols].bitcast(F32), start=k == 0, stop=False)
                        last = nc.tensor.matmul(zf[:, f, :HALF], wf[:, k], xlo[:, k, cols].bitcast(F32),
                                                start=False, stop=k == KD - 1)
                last.then_inc(f_mm, 1)
                on_tensor(pe)
                pe.wait_ge(f_dve, 9)
                for t in range(TT):
                    r = rows(t)
                    last = nc.tensor.transpose(lp[:r, t], logf[:, t * P:t * P + r], ident[:NH, :NH])
                last.then_inc(f_mm, 1)
        proj.close()

        o = sb(attn, "o", [P, TT, D])
        NPG = PAST // PAGE
        GB = 4
        UC = PAST + NS
        paged = ExitStack()
        qd = sb(paged, "qd", [P, 2, 4, DEC_B, NS])
        kc = sb(paged, "kc", [P, DEC_B, 4, PAST])
        vc = sb(paged, "vc", [P, DEC_B, NPG, 512])
        pt = sb(paged, "pt", [1, DEC_B * NPG], mybir.dt.int32)
        T = sb(paged, "T", [P, 4, UC])
        lg = sb(paged, "lg", [P, 2, PAST + DEC_S])
        newmask = sb(paged, "newmask", [P, DEC_S])
        names = ("pt", "consts", "clear", "lg", "dil", "scan", "T", "qd", "s_mm", "l", "e", "t_mm", "et", "pv",
                 "r", "om", "os", "oev")
        sam = {n: sem("s_" + n) for n in names}
        kld = [sem(f"s_kld{g}") for g in range(DEC_B // GB)]
        vld = [sem(f"s_vld{g}") for g in range(DEC_B // GB)]
        kwin = [sem(f"s_kwin{g}") for g in range(DEC_B // GB)]
        vwin = [sem(f"s_vwin{g}") for g in range(DEC_B // GB)]
        n_pool = A["k_pages"].shape[0]
        with ExitStack() as st:
            qa = sb(st, "qa", [HD + 1, 2, SEQ])
            ka = sb(st, "ka", [HD + 1, 2, SEQ])
            vh = sb(st, "vh", [P, 2, TT - 1, HD])
            bt = sb(st, "bt", [P, 2, SEQ])
            L = sb(st, "L", [P, 2, SEQ])
            negm = sb(st, "negm", [P, 2])
            E = sb(st, "E", [P, 2, SEQ])
            ET = sb(st, "ET", [P, 2, 4, P])
            den = sb(st, "den", [P, 2, 4])
            rden = sb(st, "rden", [P, 2, 4])
            S = [ps(st, f"S{i}", [P, SEQ]) for i in range(2)]
            TP = [ps(st, f"TP{i}", [P, 4, P]) for i in range(2)]
            OP = [ps(st, f"OP{i}", [P, 4, HD]) for i in range(2)]
            stg = [sem(f"a_stg{u}") for u in range(2)]
            s_mm, l_done, e_done, t_mm2, t_ev2, pv_mm, r_done, o_ev, one = (
                sem("a_" + n) for n in ("s_mm", "l_done", "e_done", "t_mm", "t_ev", "pv_mm", "r_done", "o_ev", "one"))
            block = st.enter_context(nc.Block())
            QB = TT - 1
            steps = [(u, qb) for u in range(2) for qb in range(QB)]

            def later(stage, j, i, last):
                if i < len(steps):
                    stage(j, i)
                elif not last:
                    stage(j + 1, i - len(steps))

            @block.gpsimd
            def _(pool):
                nc.gpsimd.memset(qd[:], 0.0).then_inc(sam["clear"], 1)
                nc.gpsimd.memset(T[:], NEG).then_inc(sam["clear"], 1)
                pool.wait_ge(sam["pt"], 16)
                for b in range(DEC_B):
                    g, bi = b // GB, b % GB
                    for i in range(NPG):
                        page = pool.value_load(pt[0:1, b * NPG + i:b * NPG + i + 1], min_val=0, max_val=n_pool - 1)
                        pool.dma_start(kc[:, b, :, i * PAGE:(i + 1) * PAGE], A["k_pages"][page]).then_inc(kld[g], 16)
                        pool.dma_start(vc[:, b, i], A["v_pages"][page]).then_inc(vld[g], 16)
                        src = A["logf_pages"][page].unsqueeze(1).broadcast_to([NH, DEC_S, PAGE])
                        pool.dma_start(lg[NS * bi:NS * (bi + 1), g, i * PAGE:(i + 1) * PAGE], src).then_inc(sam["lg"], 16)
                    new = bass.AP(logf_dram.tensor, SEQ + b * DEC_S, [[NT, NH], [0, DEC_S], [1, DEC_S]])
                    pool.dma_start(lg[NS * bi:NS * (bi + 1), g, PAST:], new).then_inc(sam["lg"], 16)
                pool.wait_ge(sam["clear"], 2)
                for g in range(DEC_B // GB):
                    for bi in range(GB):
                        rws = slice(NS * bi, NS * (bi + 1))
                        past = bass.AP(bias_dram.tensor, NH * DIST + SEQ - 1 - PAST, [[DIST, NH], [-1, DEC_S], [1, PAST]])
                        pool.dma_start(T[rws, 2 + g, :PAST], past).then_inc(sam["dil"], 16)
                        new = bass.AP(bias_dram.tensor, NH * DIST + SEQ - 1, [[DIST, NH], [-1, DEC_S], [1, DEC_S]])
                        c0 = PAST + DEC_S * (GB * g + bi)
                        pool.dma_start(T[rws, 2 + g, c0:c0 + DEC_S], new).then_inc(sam["dil"], 16)
                for bi in range(GB):
                    future = bass.AP(bias_dram.tensor, SEQ - 1, [[DIST, NH], [-1, DEC_S], [1, DEC_S]])
                    pool.dma_start(newmask[NS * bi:NS * (bi + 1)], future).then_inc(sam["dil"], 16)
                for kind in range(2):
                    for c in range(4):
                        for u in range(2):
                            hh = 2 * c + u
                            src = qkT[u * HD:(u + 1) * HD, 2 * (kind * 4 + c), SEQ:].rearrange("p (b q) -> p b q", b=DEC_B)
                            nc.gpsimd.tensor_copy(qd[u * HD:(u + 1) * HD, kind, c, :, hh * DEC_S:(hh + 1) * DEC_S],
                                                  src).then_inc(sam["qd"], 1)

            @block.sync
            def _(sp):
                sp.dma_start(pt[:], A["page_table"]).then_inc(sam["pt"], 16)
                sp.wait_ge(tiles_done, 16)
                with sp.Fori(0, PAIRS) as j:
                    for u in range(2):
                        sp.wait_ge(o_ev, 2 * j + u + 1)
                        sp.dma_start(qa[:HD, u, :], qkT[u * HD:(u + 1) * HD, 2 * j, :SEQ]).then_inc(stg[u], 16)
                        sp.dma_start(ka[:HD, u, :], qkT[u * HD:(u + 1) * HD, 2 * j + 1, :SEQ]).then_inc(stg[u], 16)
                        sp.dma_start(ka[HD:HD + 1, u, :], cum_dram[bass.ds(2 * j + u, 1)]).then_inc(stg[u], 16)
                        sp.dma_start(vh[:, u], v[:, 0:QB, bass.ds(j * P + u * HD, HD)]).then_inc(stg[u], 16)
                        sp.dma_start(bt[:, u], tile_dram[2 * j + u]).then_inc(stg[u], 16)
                sp.wait_ge(v_out, 64)

            @block.tensor
            def _(pe):
                pe.sem_inc(t_mm2, 2)
                pe.sem_inc(pv_mm, 2)
                pe.wait_ge(one, 1)

                def scores(j, i):
                    u, qb = steps[i]
                    n = (qb + 1) * P
                    if qb == 0:
                        pe.wait_ge(stg[u], 80 * (j + 1))
                    pe.wait_ge(l_done, 8 * j + i + 1)
                    nc.tensor.matmul(S[i % 2][:, :n], qa[:, u, qb * P:(qb + 1) * P], ka[:, u, :n],
                                     start=True, stop=True).then_inc(s_mm, 1)

                def transposes(j, i):
                    u, qb = steps[i]
                    pe.wait_ge(e_done, 8 * j + i + 3)
                    pe.wait_ge(t_ev2, 8 * j + i + 1)
                    for b in range(qb + 1):
                        last = nc.tensor.transpose(TP[i % 2][:, b], E[:, i % 2, b * P:(b + 1) * P], ident[:])
                    last.then_inc(t_mm2, 1)

                def values(j, i):
                    u, qb = steps[i]
                    pe.wait_ge(t_ev2, 8 * j + i + 3)
                    if qb == 0:
                        pe.wait_ge(o_ev, 2 * j + u + 1)
                    for b in range(qb + 1):
                        last = nc.tensor.matmul(OP[u][:, qb], ET[:, i % 2, b], vh[:, u, b],
                                                start=b == 0, stop=b == qb)
                    last.then_inc(pv_mm, 1)

                def turn(j, last):
                    for i in range(len(steps)):
                        later(scores, j, i + 2, last)
                        later(transposes, j, i + 1, last)
                        values(j, i)

                scores(0, 0)
                scores(0, 1)
                transposes(0, 0)
                with pe.Fori(0, PAIRS - 1) as j:
                    turn(j, False)
                turn(PAIRS - 1, True)

            @block.vector
            def _(dve):
                dve.sem_inc(l_done, 2)
                dve.sem_inc(t_ev2, 2)
                dve.sem_inc(o_ev, 2)
                nc.vector.memset(qa[HD:HD + 1], 1.0).then_inc(one, 1)

                def logits(j, i):
                    u, qb = steps[i]
                    n = (qb + 1) * P
                    dve.wait_ge(e_done, 8 * j + i + 1)
                    dve.wait_ge(s_mm, 8 * j + i + 1)
                    settle(dve)
                    nc.vector.tensor_tensor_reduce(
                        out=L[:, i % 2, :n], in0=S[i % 2][:, :n], in1=bt[:, u, SEQ - n:], scale=-1.0 / SCALE8,
                        scalar=3.0e38, op0=ALU.add, op1=ALU.min, accum_out=negm[:, i % 2:i % 2 + 1]).then_inc(l_done, 1)

                def keep_transposed(j, i):
                    u, qb = steps[i]
                    dve.wait_ge(t_mm2, 8 * j + i + 3)
                    dve.wait_ge(pv_mm, 8 * j + i + 1)
                    nc.vector.tensor_copy(ET[:, i % 2, :qb + 1], TP[i % 2][:, :qb + 1]).then_inc(t_ev2, 1)

                def turn(j, last):
                    for i, (u, qb) in enumerate(steps):
                        later(logits, j, i + 2, last)
                        later(keep_transposed, j, i + 1, last)
                        if qb == QB - 1:
                            nc.vector.reciprocal(rden[:, u], den[:, u]).then_inc(r_done, 1)
                            dve.wait_ge(r_done, 2 * j + u + 1)
                            dve.wait_ge(pv_mm, 8 * j + i + 3)
                            nc.vector.tensor_tensor(o[:, 0:QB, bass.ds(j * P + u * HD, HD)], OP[u][:],
                                                    rden[:, u].unsqueeze(2).broadcast_to([P, QB, HD]),
                                                    ALU.mult).then_inc(o_ev, 1)

                logits(0, 0)
                logits(0, 1)
                keep_transposed(0, 0)
                with dve.Fori(0, PAIRS - 1) as j:
                    turn(j, False)
                turn(PAIRS - 1, True)

            @block.scalar
            def _(act):
                act.sem_inc(e_done, 2)
                with act.Fori(0, PAIRS) as j:
                    for i, (u, qb) in enumerate(steps):
                        n = (qb + 1) * P
                        if qb == 0:
                            act.wait_ge(o_ev, 2 * j + u + 1)
                        act.wait_ge(l_done, 8 * j + i + 3)
                        act.wait_ge(t_mm2, 8 * j + i + 1)
                        nc.scalar.activation(E[:, i % 2, :n], L[:, i % 2, :n], ACT.Exp, bias=negm[:, i % 2:i % 2 + 1],
                                             scale=-1.0, accum_out=den[:, u, qb:qb + 1]).then_inc(e_done, 1)

        with ExitStack() as st:
            ones = sb(st, "sones", [P, PAST + DEC_S])
            hmask = sb(st, "hmask", [P, NH])
            sel = sb(st, "sel", [P, 2, NS])
            L = sb(st, "sL", [P, 2, UC])
            E = sb(st, "sE", [P, 2, UC])
            ET = sb(st, "sET", [P, 2, NPG + 1, P])
            negm = sb(st, "snegm", [P, 4])
            den = sb(st, "sden", [P, 4])
            rden = sb(st, "srden", [P, 4])
            Om = sb(st, "sOm", [P, 2, 512])
            S = [ps(st, f"sS{i}", [P, UC]) for i in range(2)]
            TP = [ps(st, f"sTP{i}", [P, NPG + 1, P]) for i in range(2)]
            OP = [ps(st, f"sOP{i}", [P, 512]) for i in range(2)]
            OS = [ps(st, f"sOS{i}", [NS, 512]) for i in range(2)]
            s = sam
            block = st.enter_context(nc.Block())
            units = [(kind, g) for kind in range(2) for g in range(DEC_B // GB)]

            @block.sync
            def _(sp):
                sp.dma_start(hmask[:], A["head_mask"]).then_inc(s["consts"], 16)
                sp.dma_start(sel[:], A["row_select"]).then_inc(s["consts"], 16)
                for b in range(DEC_B):
                    sp.wait_ge(s["s_mm"], b // GB + 1)
                    sp.dma_start(kc[:, b], A["k_win"][b]).then_inc(kwin[b // GB], 16)
                for b in range(DEC_B):
                    sp.wait_ge(s["pv"], b // GB + 1)
                    sp.dma_start(vc[:, b], A["v_win"][b].rearrange("(i p) n -> p i n", p=P)).then_inc(vwin[b // GB], 16)

            @block.vector
            def _(dve):
                nc.vector.memset(ET[:], 0.0).then_inc(s["clear"], 1)
                nc.vector.memset(ones[:], 1.0).then_inc(s["clear"], 1)
                dve.wait_ge(s["clear"], 4)
                dve.wait_ge(s["lg"], 16 * DEC_B * (NPG + 1))
                dve.wait_ge(s["consts"], 32)
                dve.wait_ge(s["dil"], 16 * 5 * GB)
                for g in range(2):
                    nc.vector.tensor_tensor_scan(lg[:, g], ones[:], lg[:, g], 0.0, ALU.mult, ALU.add).then_inc(s["scan"], 1)
                for g in range(2):
                    dve.wait_ge(s["scan"], g + 1)
                    nc.vector.tensor_scalar(T[:, g, :PAST], lg[:, g, :PAST], -SCALE8, None, ALU.mult).then_inc(s["T"], 1)
                    for bi in range(GB):
                        rws = slice(NS * bi, NS * (bi + 1))
                        c0 = PAST + DEC_S * (GB * g + bi)
                        nc.vector.scalar_tensor_tensor(T[rws, g, c0:c0 + DEC_S], lg[rws, g, PAST:], -SCALE8, newmask[rws],
                                                       ALU.mult, ALU.add).then_inc(s["T"], 1)

                def logits(i):
                    if i == 0:
                        dve.wait_ge(s["T"], 2 * (GB + 1))
                    if i >= 2:
                        dve.wait_ge(s["e"], i - 1)
                    dve.wait_ge(s["s_mm"], i + 1)
                    nc.vector.tensor_tensor_reduce(
                        out=L[:, i % 2], in0=S[i % 2][:], in1=T[:, i], scale=-1.0 / SCALE8, scalar=3.0e38,
                        op0=ALU.add, op1=ALU.min, accum_out=negm[:, i:i + 1]).then_inc(s["l"], 1)

                logits(0)
                for i in range(4):
                    if i + 1 < 4:
                        logits(i + 1)
                    dve.wait_ge(s["t_mm"], i + 1)
                    if i >= 2:
                        dve.wait_ge(s["pv"], i - 1)
                    nc.vector.tensor_copy(ET[:, i % 2, :NPG], TP[i % 2][:, :NPG])
                    nc.vector.tensor_copy(ET[:NS, i % 2, NPG], TP[i % 2][:NS, NPG]).then_inc(s["et"], 1)
                    nc.vector.reciprocal(rden[:, i:i + 1], den[:, i:i + 1]).then_inc(s["r"], 1)
                    dve.wait_ge(s["r"], i + 1)
                    dve.wait_ge(s["pv"], i + 1)
                    if i >= 2:
                        dve.wait_ge(s["os"], i - 1)
                    nc.vector.scalar_tensor_tensor(
                        Om[:, i % 2].rearrange("p (h d) -> p h d", h=NH), OP[i % 2][:].rearrange("p (h d) -> p h d", h=NH),
                        rden[:, i:i + 1], hmask[:].unsqueeze(2).broadcast_to([P, NH, HD]), ALU.mult, ALU.mult).then_inc(s["om"], 1)

            @block.scalar
            def _(act):
                for i in range(4):
                    act.wait_ge(s["l"], i + 1)
                    if i >= 2:
                        act.wait_ge(s["t_mm"], i - 1)
                    nc.scalar.activation(E[:, i % 2], L[:, i % 2], ACT.Exp, bias=negm[:, i:i + 1], scale=-1.0,
                                         accum_out=den[:, i:i + 1]).then_inc(s["e"], 1)
                for kind in range(2):
                    act.wait_ge(s["os"], 2 * kind + 2)
                    nc.scalar.activation(o[:NS, TT - 1, kind * 512:(kind + 1) * 512], OS[kind][:], ACT.Copy).then_inc(s["oev"], 1)

            @block.tensor
            def _(pe):
                def scores(i):
                    kind, g = units[i]
                    if i == 0:
                        pe.wait_ge(s["qd"], 16)
                    if i >= 2:
                        pe.wait_ge(s["l"], i - 1)
                    for c in range(4):
                        nc.tensor.matmul(S[i % 2][:, PAST:], qd[:, kind, c, GB * g:GB * (g + 1), :],
                                         qkT[:, 2 * (kind * 4 + c) + 1, SEQ:], start=c == 0, stop=c == 3)
                    for bi in range(GB):
                        b = GB * g + bi
                        pe.wait_ge((kld, kwin)[kind][g], 16 * GB * (NPG, 1)[kind])
                        for c in range(4):
                            last = nc.tensor.matmul(S[i % 2][NS * bi:NS * (bi + 1), :PAST], qd[:, kind, c, b, :], kc[:, b, c, :],
                                                    start=c == 0, stop=c == 3)
                    last.then_inc(s["s_mm"], 1)

                def select(i):
                    kind, g = units[i]
                    pe.wait_ge(s["om"], i + 1)
                    nc.tensor.matmul(OS[kind][:], sel[:, g], Om[:, i % 2], start=g == 0, stop=g == 1).then_inc(s["os"], 1)

                scores(0)
                for i, (kind, g) in enumerate(units):
                    if i + 1 < 4:
                        scores(i + 1)
                    pe.wait_ge(s["e"], i + 1)
                    if i >= 2:
                        pe.wait_ge(s["et"], i - 1)
                    for b in range(NPG):
                        nc.tensor.transpose(TP[i % 2][:, b], E[:, i % 2, b * P:(b + 1) * P], ident[:])
                    nc.tensor.transpose(TP[i % 2][:NS, NPG], E[:, i % 2, PAST:], ident[:]).then_inc(s["t_mm"], 1)
                    pe.wait_ge(s["et"], i + 1)
                    if i >= 2:
                        pe.wait_ge(s["om"], i - 1)
                    nc.tensor.matmul(OP[i % 2][:], ET[:, i % 2, NPG], v[:, TT - 1, kind * 512:(kind + 1) * 512],
                                     start=True, stop=False, skip_group_check=True)
                    for bi in range(GB):
                        b = GB * g + bi
                        pe.wait_ge((vld, vwin)[kind][g], 16 * GB * (NPG, 1)[kind])
                        for j in range(NPG):
                            last = nc.tensor.matmul(OP[i % 2][NS * bi:NS * (bi + 1), :], ET[:, i % 2, j, NS * bi:NS * (bi + 1)],
                                                    vc[:, b, j], start=False, stop=j == NPG - 1, skip_group_check=True)
                    last.then_inc(s["pv"], 1)
                    if i >= 1:
                        select(i - 1)
                select(3)

        paged.close()

        with ExitStack() as late:
            w_early = sb(late, "po_w", [P, 2, KD, 256])
            w_loaded = [sem(f"po_wld{u}") for u in range(2)]
            ohi = sb(late, "ohi", [P, KD, NTP], F32R)
            olo = sb(late, "olo", [P, KD, NTP], F32R)
            
            def load_w_out(sp, loaded):
                for u in range(2):
                    sp.dma_start(w_early[:, u], A["w_out"][u]).then_inc(w_loaded[u], 16)

            norm_stage("no", o, 2, A["g_out"], ohi, olo, (0, load_w_out))
            with ExitStack() as st:
                def add_to_h(t, chunk, acc):
                    r = rows(t)
                    cols = bass.ds(chunk * 256, 256)
                    return nc.vector.tensor_tensor(h[:r, t, cols], h[:r, t, cols], acc[:r], ALU.add)

                on_sync, on_scalar, first_on_vector, on_vector, on_tensor = token_rows_product(st, "po", ohi, olo, w_early, w_loaded, A["w_out"], 4, add_to_h)
                block = st.enter_context(nc.Block())
                block.sync(on_sync)
                block.scalar(on_scalar)
                block.vector(lambda dve: (first_on_vector(dve), on_vector(dve)))
                block.tensor(on_tensor)
        attn.close()

        ahead = ExitStack()
        vw = sb(ahead, "vw", [P, GT, D])
        gt = sb(ahead, "gt", [P, 2, NCH, GT, CH])
        hd = sb(ahead, "hd", [P, 2, GT, NT])
        vld = [sem(f"x_vld{i}") for i in range(GT)]
        gld = [sem(f"x_gld{i}") for i in range(2)]
        query = ExitStack()
        x2hi = sb(query, "x2hi", [P, KD, NT], F32R)
        x2lo = sb(query, "x2lo", [P, KD, NT], F32R)
        norm_stage("nf", h, 1, A["g_ffn"], x2hi, x2lo)

        uw = sb(query, "uw", [P, 2, KD, P])
        uhi = sb(query, "uhi", [P, 2, KD, P], F32R)
        ulo = sb(query, "ulo", [P, 2, KD, P], F32R)
        ge = sb(query, "gelu_out", [P, 2, NT])
        hp = [ps(query, f"hp{i}", [P, 2, SEQ]) for i in range(2)]
        u_load = [sem(f"u_load{i}") for i in range(2)]
        ge_stored = [sem(f"ge_stored{i}") for i in range(2)]
        u_hi, u_lo, h_mm, gelu_done = (sem(n) for n in ("u_hi", "u_lo", "h_mm", "gelu_done"))

        def u_fetch(sp, m, i):
            sp.wait_ge(u_lo, m + 1)
            sp.dma_start(uw[:, i], A["u_experts"][m]).then_inc(u_load[i], 16)

        def u_split_hi(act, m, i):
            act.wait_ge(u_load[i], (m - i) * 8 + 16)
            act.wait_ge(h_mm, m + 1)
            nc.scalar.activation(uhi[:, i], uw[:, i], ACT.Copy).then_inc(u_hi, 1)

        def u_split_lo(pool, m, i):
            pool.wait_ge(u_hi, m + 1)
            nc.gpsimd.tensor_tensor(ulo[:, i], uw[:, i], uhi[:, i].bitcast(F32), ALU.subtract).then_inc(u_lo, 1)

        def hidden_product(pe, m, i):
            pe.wait_ge(u_lo, m + 3)
            pe.wait_ge(gelu_done, m + 1)
            for k in range(KD):
                for f in range(2):
                    cols = slice(f * HALF, (f + 1) * HALF)
                    last = mm3(hp[i][:, f, :HALF], uhi[:, i, k], ulo[:, i, k], x2hi[:, k, cols], x2lo[:, k, cols],
                               k == 0, k == KD - 1)
            last.then_inc(h_mm, 1)

        def hidden_gelu(act, m, i):
            act.wait_ge(h_mm, m + 3)
            act.wait_ge(ge_stored[i], (m - i) * 8 + 16)
            nc.scalar.activation(ge[:, i].rearrange("p (a b) -> p a b", a=2), hp[i][:, :, :HALF], ACT.Gelu).then_inc(gelu_done, 1)
            act.wait_ge(gelu_done, m + 3)
            act.dma_start(gelu_dram[m], ge[:, i]).then_inc(ge_stored[i], 16)

        RT = 4
        QX, GX = 8, 8
        GTI = (NK - RT * NH - QX - GX) // (NCH // 2)
        G0 = RT * NH + QX
        assert G0 + GTI * (NCH // 2) + GX == NK and GTI % 2 == 0 and QX % 4 == 0 and GX % 2 == 0

        def load_gates(sp, g, par):
            sp.dma_start(hd[:, par], gelu_dram[bass.ds(g * GT, GT)].rearrange("i p t -> p i t")).then_inc(gld[par], 16)
            sp.dma_start(gt[:, par].rearrange("p c i t -> p c (i t)"),
                         gate_dram[:, :, bass.ds(g * GT, GT), :].rearrange("c p i t -> p c (i t)")).then_inc(gld[par], 16)

        pick = ExitStack()
        I1 = sb(pick, "I1", [P, TT, P])
        I2 = sb(pick, "I2", [P, TT, P])
        GG = sb(pick, "GG", [P, TT, P])
        iota = sb(pick, "iota", [P, P])
        TK = TT * TOPK
        with ExitStack() as st:
            w = sb(st, "qw", [P, 2, KD, P])
            whi = sb(st, "qwhi", [P, 2, KD, P], F32R)
            wlo = sb(st, "qwlo", [P, 2, KD, P], F32R)
            qT = sb(st, "qT", [P, 2, NT])
            keys = sb(st, "keys", [P, 2, NK])
            sc = sb(st, "sc", [P, 2, TT, NK])
            sc2 = sb(st, "sc2", [P, 2, TT, NK])
            V8 = sb(st, "V8", [P, 2, TT, TOPK])
            X8 = sb(st, "X8", [P, 2, TT, TOPK], U32)
            XF = sb(st, "XF", [P, 2, TT, TOPK])
            cand = sb(st, "cand", [P, TT, TOPK, TOPK])
            cand2 = sb(st, "cand2", [P, TT, TOPK * TOPK])
            top = sb(st, "top", [P, TT, TOPK])
            pos = sb(st, "pos", [P, TT, TOPK], U32)
            ab = sb(st, "ab", [P, 2, TT, TOPK], U32)
            abf = sb(st, "abf", [P, 2, TT, TOPK])
            eq = sb(st, "eq", [P, 2, TT, TOPK, TOPK])
            pk = sb(st, "pk", [P, 2, TT, TOPK])
            sm = sb(st, "sm", [P, TT * NH])
            first = sb(st, "first", [P, TT * NH])
            zp = ps(st, "qzp", [P, 2, SEQ])
            sp_ = ps(st, "qsp", [P, 8, NK])
            wld = [sem(f"q_wld{u}") for u in range(2)]
            names = ("c", "hi", "lo", "mm", "ev", "smm", "sev", "read", "topk", "exin", "ex", "sum", "chain", "clr")
            s = {n: sem("q_" + n) for n in names}
            block = st.enter_context(nc.Block())

            @block.sync
            def _(sp):
                sp.dma_start(keys[:], A["sub_keys"]).then_inc(s["c"], 16)
                sp.dma_start(iota[:], A["iota"]).then_inc(s["c"], 16)
                with sp.Fori(0, NH) as j:
                    for u in range(2):
                        sp.wait_ge(s["lo"], 2 * j + u + 1)
                        sp.dma_start(w[:, u], A["w_query"][2 * j + u]).then_inc(wld[u], 16)
                        for i in range(2):
                            u_fetch(sp, RT * j + 2 * u + i, i)
                with sp.Fori(0, QX // 2 + 1) as e:
                    for i in range(2):
                        u_fetch(sp, RT * NH + 2 * e + i, i)

            @block.gpsimd
            def _(pool):
                pool.sem_inc(s["lo"], 2)
                pool.sem_inc(u_lo, 2)

                def split(n, u):
                    pool.wait_ge(s["hi"], n + 1)
                    nc.gpsimd.tensor_tensor(wlo[:, u], w[:, u], whi[:, u].bitcast(F32), ALU.subtract).then_inc(s["lo"], 1)

                def turn(j, last):
                    for u in range(2):
                        u_split_lo(pool, RT * j + 2 + u, u)
                        if not last:
                            split(2 * j + 2 + u, u)
                    for i in range(2):
                        u_split_lo(pool, RT * j + RT + i, i)

                split(0, 0)
                split(1, 1)
                u_split_lo(pool, 0, 0)
                u_split_lo(pool, 1, 1)
                with pool.Fori(0, NH - 1) as j:
                    turn(j, False)
                turn(NH - 1, True)
                with pool.Fori(0, QX // 2) as e:
                    for i in range(2):
                        u_split_lo(pool, RT * NH + 2 * e + i + 2, i)

            @block.scalar
            def _(act):
                act.sem_inc(s["ev"], 1)
                act.sem_inc(s["sev"], 1)
                act.sem_inc(gelu_done, 2)
                act.sem_inc(ge_stored[0], 16)
                act.sem_inc(ge_stored[1], 16)
                act.wait_ge(s["clr"], 1)

                def split(n, u, j):
                    act.wait_ge(wld[u], 16 * j + 16)
                    act.wait_ge(s["mm"], n + 1)
                    nc.scalar.activation(whi[:, u], w[:, u], ACT.Copy).then_inc(s["hi"], 1)

                def turn(j, last):
                    for u in range(2):
                        n = 2 * j + u
                        act.wait_ge(s["mm"], n + 3)
                        act.wait_ge(s["smm"], n + 1)
                        nc.scalar.activation(qT[:, u].rearrange("p (a b) -> p a b", a=2), zp[:, :, :HALF],
                                             ACT.Copy).then_inc(s["ev"], 1)
                        u_split_hi(act, RT * j + 2 + u, u)
                        hidden_gelu(act, RT * j + u, u)
                        act.wait_ge(s["smm"], n + 3)
                        act.wait_ge(s["read"], j + 1)
                        nc.scalar.activation(sc[:, u, 0:TT - 1], sp_[:, 0:TT - 1], ACT.Copy)
                        nc.scalar.activation(sc[:NS, u, TT - 1], sp_[:NS, TT - 1], ACT.Copy).then_inc(s["sev"], 1)
                        if not last:
                            split(n + 2, u, j + 1)
                    for i in range(2):
                        u_split_hi(act, RT * j + RT + i, i)
                        hidden_gelu(act, RT * j + 2 + i, i)

                split(0, 0, 0)
                split(1, 1, 0)
                u_split_hi(act, 0, 0)
                u_split_hi(act, 1, 1)
                with act.Fori(0, NH - 1) as j:
                    turn(j, False)
                turn(NH - 1, True)
                with act.Fori(0, QX // 2) as e:
                    for i in range(2):
                        u_split_hi(act, RT * NH + 2 * e + i + 2, i)
                        hidden_gelu(act, RT * NH + 2 * e + i, i)
                act.wait_ge(s["exin"], 1)
                nc.scalar.activation(GG[:], GG[:], ACT.Exp).then_inc(s["ex"], 1)

            @block.tensor
            def _(pe):
                pe.sem_inc(s["mm"], 2)
                pe.sem_inc(s["smm"], 2)
                pe.sem_inc(h_mm, 2)
                pe.wait_ge(s["c"], 32)
                with pe.Fori(0, NH) as j:
                    for u in range(2):
                        n = 2 * j + u
                        pe.wait_ge(s["lo"], n + 3)
                        pe.wait_ge(s["ev"], n + 1)
                        for k in range(KD):
                            for f in range(2):
                                last = mm3(zp[:, f, :HALF], whi[:, u, k], wlo[:, u, k],
                                           x2hi[:, k, f * HALF:(f + 1) * HALF], x2lo[:, k, f * HALF:(f + 1) * HALF],
                                           k == 0, k == KD - 1)
                        last.then_inc(s["mm"], 1)
                        hidden_product(pe, RT * j + u, u)
                        pe.wait_ge(s["ev"], n + 2)
                        pe.wait_ge(s["sev"], n + 1)
                        for t in range(TT):
                            r = rows(t)
                            last = nc.tensor.matmul(sp_[:r, t], qT[:, u, t * P:t * P + r], keys[:, u],
                                                    start=True, stop=True)
                        last.then_inc(s["smm"], 1)
                    for i in range(2):
                        hidden_product(pe, RT * j + 2 + i, i)
                with pe.Fori(0, QX // 2) as e:
                    for i in range(2):
                        hidden_product(pe, RT * NH + 2 * e + i, i)

            @block.vector
            def _(dve):
                nc.vector.memset(sc[:], 0.0).then_inc(s["clr"], 1)
                dve.sem_inc(s["read"], 1)
                dve.wait_ge(s["c"], 32)
                LINKS = 14
                ut = [(u, t) for u in range(2) for t in range(TT)]
                with dve.Fori(0, NH) as j:
                    links = [0]

                    def link(ins):
                        links[0] += 1
                        ins.then_inc(s["chain"], 1)
                        dve.wait_ge(s["chain"], j * LINKS + links[0])
                        settle(dve)

                    for u in range(2):
                        dve.wait_ge(s["sev"], 2 * j + u + 2)
                    settle(dve)
                    for u, t in ut:
                        last = nc.vector.max(V8[:, u, t, 0:8], sc[:, u, t])
                    link(last)
                    for u, t in ut:
                        nc.vector.max_index(X8[:, u, t, 0:8], V8[:, u, t, 0:8], sc[:, u, t])
                        last = nc.vector.match_replace(sc2[:, u, t], V8[:, u, t, 0:8], sc[:, u, t], -3.0e38)
                    link(last)
                    dve.sem_inc(s["read"], 1)
                    for u, t in ut:
                        last = nc.vector.max(V8[:, u, t, 8:16], sc2[:, u, t])
                    link(last)
                    for u, t in ut:
                        last = nc.vector.max_index(X8[:, u, t, 8:16], V8[:, u, t, 8:16], sc2[:, u, t])
                    link(last)
                    nc.vector.tensor_copy(XF[:], X8[:])
                    link(nc.vector.tensor_tensor(cand[:], V8[:, 0].unsqueeze(3).broadcast_to([P, TT, TOPK, TOPK]),
                                                 V8[:, 1].unsqueeze(2).broadcast_to([P, TT, TOPK, TOPK]), ALU.add))
                    flat = [cand[:, t].rearrange("p a b -> p (a b)") for t in range(TT)]
                    for t in range(TT):
                        last = nc.vector.max(top[:, t, 0:8], flat[t])
                    link(last)
                    for t in range(TT):
                        nc.vector.max_index(pos[:, t, 0:8], top[:, t, 0:8], flat[t])
                        last = nc.vector.match_replace(cand2[:, t], top[:, t, 0:8], flat[t], -3.0e38)
                    link(last)
                    for t in range(TT):
                        last = nc.vector.max(top[:, t, 8:16], cand2[:, t])
                    link(last)
                    for t in range(TT):
                        last = nc.vector.max_index(pos[:, t, 8:16], top[:, t, 8:16], cand2[:, t])
                    link(last)
                    nc.vector.tensor_scalar(ab[:, 0], pos[:], 4, None, ALU.logical_shift_right)
                    link(nc.vector.tensor_scalar(ab[:, 1], pos[:], 15, None, ALU.bitwise_and))
                    link(nc.vector.tensor_copy(abf[:], ab[:]))
                    ranks = iota[:, 0:TOPK].unsqueeze(1).broadcast_to([P, 2 * TK, TOPK])
                    link(nc.vector.tensor_tensor(eq[:].rearrange("p u t k a -> p (u t k) a"), ranks,
                                                 abf[:].rearrange("p u t k -> p (u t k)").unsqueeze(2).broadcast_to([P, 2 * TK, TOPK]),
                                                 ALU.is_equal))
                    for u in range(2):
                        last = nc.vector.tensor_tensor(eq[:, u], eq[:, u], XF[:, u].unsqueeze(2).broadcast_to([P, TT, TOPK, TOPK]),
                                                       ALU.mult)
                    link(last)
                    link(nc.vector.tensor_reduce(pk[:], eq[:], axis=AX.X, op=ALU.add))
                    assert links[0] == LINKS, links[0]
                    nc.vector.tensor_copy(GG[:, :, bass.ds(j * TOPK, TOPK)], top[:])
                    nc.vector.tensor_copy(I1[:, :, bass.ds(j * TOPK, TOPK)], pk[:, 0])
                    nc.vector.tensor_copy(I2[:, :, bass.ds(j * TOPK, TOPK)], pk[:, 1]).then_inc(s["topk"], 1)
                heads = GG[:].rearrange("p t (h k) -> p (t h) k", k=TOPK)
                dve.wait_ge(s["topk"], NH)
                nc.vector.tensor_copy(first[:].unsqueeze(2), heads[:, :, 0:1]).then_inc(s["sum"], 1)
                dve.wait_ge(s["sum"], 1)
                nc.vector.tensor_tensor(heads, heads, first[:].unsqueeze(2).broadcast_to([P, TT * NH, TOPK]),
                                        ALU.subtract).then_inc(s["exin"], 1)
                dve.wait_ge(s["ex"], 1)
                nc.vector.tensor_reduce(sm[:], heads, axis=AX.X, op=ALU.add).then_inc(s["sum"], 1)
                dve.wait_ge(s["sum"], 2)
                nc.vector.reciprocal(sm[:], sm[:]).then_inc(s["sum"], 1)
                dve.wait_ge(s["sum"], 3)
                nc.vector.tensor_tensor(heads, heads, sm[:].unsqueeze(2).broadcast_to([P, TT * NH, TOPK]), ALU.mult)

        with ExitStack() as st:
            slotT = sb(st, "slotT", [P, 3, NT])
            gthi = sb(st, "gthi", [P, NT], F32R)
            chunkT = sb(st, "chunkT", [P, 2, 4, CH])
            oh = sb(st, "oh", [P, 2, 4, P], F32R)
            ogh = sb(st, "ogh", [P, 2, 4, P], F32R)
            ogl = sb(st, "ogl", [P, 2, 4, P], F32R)
            gst = sb(st, "gst", [P, 2, NK, CH])
            gp = [ps(st, f"ggp{i}", [P, 4, P]) for i in range(2)]
            tp = ps(st, "gtp", [P, 2, SEQ])
            names = ("tr", "trev", "ghi", "glo", "cut", "oh", "mm", "ev", "part")
            s = {n: sem("g_" + n) for n in names}
            stored = [sem(f"g_stored{u}") for u in range(2)]
            block = st.enter_context(nc.Block())
            sizes = [4] * (CH // 4) + [CH % 4] * (CH % 4 > 0)
            GR = len(sizes)
            groups = [(u, r) for u in range(2) for r in range(GR)]
            N2 = 2 * GR
            NI = NCH // 2

            def interleave(tile, group):
                at = 0
                for i in range(GTI):
                    tile(i)
                    upto = N2 * (i + 1) // GTI
                    while at < upto:
                        group(at)
                        at += 1

            @block.tensor
            def _(pe):
                for i, src in enumerate((I1, I2, GG)):
                    if i:
                        pe.wait_ge(s["trev"], i)
                    for t in range(TT):
                        r = rows(t)
                        last = nc.tensor.transpose(tp[:, t // 4, (t % 4) * P:(t % 4) * P + r], src[:r, t], ident[:r, :r])
                    last.then_inc(s["tr"], 1)
                pe.sem_inc(s["mm"], 2)
                with pe.Fori(0, NI) as j:
                    def group(i):
                        u, r = groups[i]
                        pe.wait_ge(s["oh"], j * N2 + i + 1)
                        pe.wait_ge(s["ev"], j * N2 + i + 1)
                        for k in range(sizes[r]):
                            nc.tensor.matmul(gp[i % 2][:, k], oh[:, i % 2, k], ogh[:, i % 2, k], start=True, stop=False)
                            last = nc.tensor.matmul(gp[i % 2][:, k], oh[:, i % 2, k], ogl[:, i % 2, k], start=False, stop=True)
                        last.then_inc(s["mm"], 1)

                    interleave(lambda i: hidden_product(pe, G0 + GTI * j + i, i % 2), group)
                with pe.Fori(0, GX // 2) as e:
                    for i in range(2):
                        hidden_product(pe, NK - GX + 2 * e + i, i)

            @block.gpsimd
            def _(pool):
                pool.wait_ge(s["glo"], 1)

                def cut(j, u):
                    pool.wait_ge(s["part"], 2 * j + u + 1)
                    cols = bass.ds((2 * j + u) * CH, CH)
                    nc.gpsimd.tensor_copy(chunkT[:, u, 0:3], slotT[:, :, cols])
                    nc.gpsimd.tensor_copy(chunkT[:, u, 3], gthi[:, cols].bitcast(F32)).then_inc(s["cut"], 1)

                def turn(j, last):
                    for i in range(GTI):
                        if i == 1:
                            cut(j, 1)
                        if i == GTI // 2 + 2 and not last:
                            cut(j + 1, 0)
                        u_split_lo(pool, G0 + GTI * j + i + 2, i % 2)

                cut(0, 0)
                with pool.Fori(0, NI - 1) as j:
                    turn(j, False)
                turn(NI - 1, True)
                with pool.Fori(0, GX // 2 - 1) as e:
                    for i in range(2):
                        u_split_lo(pool, NK - GX + 2 * e + i + 2, i)

            @block.vector
            def _(dve):
                dve.sem_inc(s["part"], 2)
                dve.wait_ge(s["ghi"], 1)
                nc.vector.tensor_tensor(slotT[:, 2], slotT[:, 2], gthi[:].bitcast(F32), ALU.subtract).then_inc(s["glo"], 1)
                with dve.Fori(0, NI) as j:
                    for i, (u, r) in enumerate(groups):
                        if r == 0:
                            dve.wait_ge(s["cut"], 2 * j + u + 1)
                        dve.wait_ge(s["mm"], j * N2 + i + 1)
                        for k in range(sizes[r]):
                            c = 4 * r + k
                            col = lambda q: chunkT[:, u, q, c:c + 1]
                            nc.vector.tensor_scalar(oh[:, i % 2, k], iota[:], col(1), None, ALU.is_equal)
                            nc.vector.tensor_scalar(ogh[:, i % 2, k], iota[:], col(0), col(3), ALU.is_equal, ALU.mult)
                            last = nc.vector.tensor_scalar(ogl[:, i % 2, k], iota[:], col(0), col(2), ALU.is_equal, ALU.mult)
                        last.then_inc(s["oh"], 1)
                        if r == GR - 1:
                            dve.wait_ge(s["oh"], j * N2 + i + 1)
                            dve.sem_inc(s["part"], 1)

            @block.scalar
            def _(act):
                for i in range(3):
                    act.wait_ge(s["tr"], i + 1)
                    nc.scalar.activation(slotT[:, i, :SEQ], tp[:, 0], ACT.Copy)
                    nc.scalar.activation(slotT[:, i, SEQ:], tp[:, 1, :NS], ACT.Copy).then_inc(s["trev"], 1)
                act.wait_ge(s["trev"], 3)
                nc.scalar.activation(gthi[:], slotT[:, 2], ACT.Copy).then_inc(s["ghi"], 1)
                act.sem_inc(s["ev"], 2)
                act.sem_inc(stored[0], 16)
                act.sem_inc(stored[1], 16)

                with act.Fori(0, NI) as j:
                    def tile(i):
                        m = G0 + GTI * j + i
                        hidden_gelu(act, m, i % 2)
                        u_split_hi(act, m + 2, i % 2)

                    def group(i):
                        u, r = groups[i]
                        if r == 0:
                            act.wait_ge(stored[u], 16 * j + 16)
                        act.wait_ge(s["mm"], j * N2 + i + 3)
                        n = sizes[r]
                        nc.scalar.activation(gst[:, u, :, 4 * r:4 * r + n], gp[i % 2][:, :n].rearrange("p t i -> p i t"),
                                             ACT.Copy).then_inc(s["ev"], 1)
                        if r == GR - 1:
                            act.wait_ge(s["ev"], j * N2 + i + 3)
                            act.dma_start(gate_dram[2 * j + u], gst[:, u]).then_inc(stored[u], 16)

                    interleave(tile, group)

                with act.Fori(0, GX // 2 - 1) as e:
                    for i in range(2):
                        u_split_hi(act, NK - GX + 2 * e + i + 2, i)
                        hidden_gelu(act, NK - GX + 2 * e + i, i)
                for i in range(2):
                    hidden_gelu(act, NK - 2 + i, i)
                for i in range(2):
                    act.wait_ge(ge_stored[i], 8 * NK + 16)

            @block.sync
            def _(sp):
                for i in range(GT):
                    sp.dma_start(vw[:, i], A["v_experts"][i]).then_inc(vld[i], 16)
                with sp.Fori(0, NI) as j:
                    for i in range(GTI):
                        u_fetch(sp, G0 + GTI * j + i + 2, i % 2)
                with sp.Fori(0, GX // 2 - 1) as e:
                    for i in range(2):
                        u_fetch(sp, NK - GX + 2 * e + i + 2, i)
                for u in range(2):
                    sp.wait_ge(stored[u], 16 * (NI + 1))
                    sp.wait_ge(ge_stored[u], 8 * G0)
                for g in range(2):
                    load_gates(sp, g, g)
        pick.close()
        query.close()

        peer = ExitStack()
        acc = sb(peer, "acc", [P, KD, NT])
        with ExitStack() as st:
            vhi = sb(st, "vhi", [P, 2, GT, D], F32R)
            vlo = sb(st, "vlo", [P, 2, GT, D], F32R)
            af = sb(st, "af", [P, 2, NT])
            ahi = sb(st, "ahi", [P, 2, GT, NT], F32R)
            alo = sb(st, "alo", [P, 2, GT, NT], F32R)
            VP = 4
            vp = [ps(st, f"vp{i}", [P, 2, SEQ]) for i in range(VP)]
            names = ("a", "ahi", "alo", "vhi", "vlo", "vmm", "acc", "clear")
            s = {n: sem("x_" + n) for n in names}
            block = st.enter_context(nc.Block())

            def over_groups(eng, step):
                with eng.Fori(0, NG // 2 - 1) as j:
                    for u in range(2):
                        step(2 * j + u, u, False)
                step(NG - 2, 0, False)
                step(NG - 1, 1, True)

            @block.sync
            def _(sp):
                def tiles(g):
                    for i in range(GT):
                        sp.wait_ge(s["vlo"], g * GT + i + 1)
                        sp.dma_start(vw[:, i], A["v_experts"][g * GT + i]).then_inc(vld[i], 16)

                tiles(1)
                with sp.Fori(0, NG // 2 - 1) as j:
                    for u in range(2):
                        g = 2 * j + u + 2
                        sp.wait_ge(s["a"], (g + 1) * GT)
                        load_gates(sp, g, u)
                        tiles(g)

            @block.scalar
            def _(act):
                def prepare(g, par, i):
                    m = g * GT + i
                    if i == 0 and not (isinstance(g, int) and g == 0):
                        act.wait_ge(s["vmm"], g * KD)
                    act.wait_ge(vld[i], 16 * g + 16)
                    nc.scalar.activation(vhi[:, par, i], vw[:, i], ACT.Copy).then_inc(s["vhi"], 1)
                    act.wait_ge(s["a"], m + 1 + 2 * GT)
                    nc.scalar.activation(ahi[:, par, i], af[:, i % 2], ACT.Copy).then_inc(s["ahi"], 1)

                def step(g, par, last):
                    if not last:
                        for i in range(GT):
                            prepare(g + 1, 1 - par, i)

                for i in range(GT):
                    prepare(0, 0, i)
                over_groups(act, step)

            @block.vector
            def _(dve):
                def prepare(g, par, i):
                    m = g * GT + i
                    dve.wait_ge(s["vhi"], m + 1)
                    nc.vector.tensor_tensor(vlo[:, par, i], vw[:, i], vhi[:, par, i].bitcast(F32), ALU.subtract).then_inc(s["vlo"], 1)
                    if i == 0:
                        dve.wait_ge(gld[par], (g - par) * 16 + 32)
                    dve.wait_ge(s["ahi"], m + 1)
                    dve.wait_ge(s["alo"], m + 1)
                    nc.vector.tensor_tensor(af[:, i % 2].rearrange("p (c t) -> p c t", c=NCH),
                                            hd[:, par, i].rearrange("p (c t) -> p c t", c=NCH),
                                            gt[:, par, :, i], ALU.mult).then_inc(s["a"], 1)
                    dve.wait_ge(s["ahi"], m + 3)
                    nc.vector.tensor_tensor(alo[:, par, i], af[:, i % 2], ahi[:, par, i].bitcast(F32),
                                            ALU.subtract).then_inc(s["alo"], 1)

                def step(g, par, last):
                    for k in range(KD):
                        dve.wait_ge(s["vmm"], g * KD + k + 1 + KD)
                        dst = acc[:, k].rearrange("p (a b) -> p a b", a=2)
                        nc.vector.tensor_tensor(dst, dst, vp[k % VP][:, :, :HALF], ALU.add).then_inc(s["acc"], 1)
                        if k in PREPARE_AFTER and not last:
                            prepare(g + 1, 1 - par, PREPARE_AFTER.index(k))

                PREPARE_AFTER = (0, 2, 3, 5)
                dve.sem_inc(s["vlo"], GT)
                dve.sem_inc(s["alo"], 2)
                dve.sem_inc(s["ahi"], 2)
                dve.sem_inc(s["a"], 2 * GT)
                dve.sem_inc(s["acc"], VP)
                for i in range(GT):
                    prepare(0, 0, i)
                dve.wait_ge(s["clear"], 1)
                over_groups(dve, step)

            @block.gpsimd
            def _(pool):
                nc.gpsimd.memset(acc[:], 0.0).then_inc(s["clear"], 1)

            @block.tensor
            def _(pe):
                pe.sem_inc(s["vmm"], KD)

                def step(g, par, last):
                    for k in range(KD):
                        pe.wait_ge(s["acc"], g * KD + k + 1)
                        for i in range(GT):
                            if k == 0:
                                pe.wait_ge(s["vlo"], g * GT + i + 1 + GT)
                                pe.wait_ge(s["alo"], g * GT + i + 1 + 2)
                            for f in range(2):
                                cols = slice(f * HALF, (f + 1) * HALF)
                                ins = mm3(vp[k % VP][:, f, :HALF], vhi[:, par, i, k * P:(k + 1) * P],
                                          vlo[:, par, i, k * P:(k + 1) * P], ahi[:, par, i, cols], alo[:, par, i, cols],
                                          i == 0, i == GT - 1)
                        ins.then_inc(s["vmm"], 1)

                over_groups(pe, step)

        with ExitStack() as st:
            y = sb(st, "y", [P, TT, D])
            sq = sb(st, "fsq", [P, D])
            gf = sb(st, "gf", [P, D])
            ssq = sb(st, "fssq", [P, TT])
            root = sb(st, "froot", [P, TT])
            rtmp = sb(st, "frtmp", [P, TT])
            tp = [ps(st, f"ftp{i}", [P, KD, P]) for i in range(2)]
            names = ("ld", "tr", "sum", "sq", "ms", "root", "inv", "scaled", "y", "out", "chain")
            s = {n: sem("n_" + n) for n in names}
            block = st.enter_context(nc.Block())

            @block.tensor
            def _(pe):
                for t in range(TT):
                    r = rows(t)
                    if t >= 2:
                        pe.wait_ge(s["sum"], t - 1)
                    for k in range(KD):
                        last = nc.tensor.transpose(tp[t % 2][:r, k], acc[:, k, t * P:t * P + r], ident[:])
                    last.then_inc(s["tr"], 1)

            @block.vector
            def _(dve):
                nc.vector.memset(ssq[:], 1.0).then_inc(s["ms"], 1)
                for t in range(TT):
                    r = rows(t)
                    dve.wait_ge(s["tr"], t + 1)
                    nc.vector.tensor_tensor(h[:r, t], h[:r, t], tp[t % 2][:r].rearrange("p k n -> p (k n)"), ALU.add).then_inc(s["sum"], 1)
                dve.wait_ge(s["sq"], TT)
                nc.vector.tensor_scalar(ssq[:], ssq[:], 1.0 / D, EPS, ALU.mult, ALU.add).then_inc(s["ms"], 1)
                dve.wait_ge(s["root"], 1)
                rsqrt_refined(dve, ssq, root, rtmp, s["chain"]).then_inc(s["inv"], 1)
                dve.wait_ge(s["ld"], 16)
                for t in range(TT):
                    r = rows(t)
                    dve.wait_ge(s["scaled"], t + 1)
                    nc.vector.tensor_tensor(y[:r, t], y[:r, t], gf[:r], ALU.mult).then_inc(s["y"], 1)

            @block.scalar
            def _(act):
                act.wait_ge(s["ms"], 1)
                for t in range(TT):
                    r = rows(t)
                    act.wait_ge(s["sum"], t + 1)
                    if t:
                        act.wait_ge(s["sq"], t)
                    nc.scalar.activation(sq[:r], h[:r, t], ACT.Square, accum_out=ssq[:r, t:t + 1]).then_inc(s["sq"], 1)
                act.wait_ge(s["ms"], 2)
                nc.scalar.activation(root[:], ssq[:], ACT.Sqrt).then_inc(s["root"], 1)
                act.wait_ge(s["inv"], 1)
                for t in range(TT):
                    r = rows(t)
                    nc.scalar.activation(y[:r, t], h[:r, t], ACT.Copy, scale=ssq[:r, t:t + 1]).then_inc(s["scaled"], 1)

            @block.sync
            def _(sp):
                sp.dma_start(gf[:], A["g_final"].broadcast_to([P, D])).then_inc(s["ld"], 16)
                sp.wait_ge(s["y"], TT - 1)
                sp.dma_start(O["y_prompt"].rearrange("(t p) d -> p t d", p=P), y[:, 0:TT - 1]).then_inc(s["out"], 16)
                sp.wait_ge(s["y"], TT)
                sp.dma_start(O["y_sample"], y[:NS, TT - 1]).then_inc(s["out"], 16)
                sp.wait_ge(s["out"], 32)
        peer.close()
        ahead.close()
        persistent.close()


def bucket(dist):
    exact = NBK // 2
    d = np.maximum(dist, 1).astype(np.float32)
    large = exact + (np.log(d / exact) / math.log(2048 / exact) * (NBK - exact)).astype(np.int32)
    return np.where(dist < exact, dist, np.minimum(large, NBK - 1))


def bias_row_constants():
    dist = SEQ - 1 - np.arange(DIST)
    count = sum(((dist >= 0) & (dist <= window) & (dist % dil == 0)).astype(np.float32)
                for window, dil in ((128, 1), (512, 4), (2048, 16)))
    out = np.zeros((NBK + 2, DIST), np.float32)
    back = dist >= 0
    out[bucket(np.maximum(dist, 0))[back], np.arange(DIST)[back]] = 1.0
    out[NBK] = np.where(count > 0, np.log(np.maximum(count, 1)), NEG)
    out[NBK + 1] = np.where(back, 0.0, NEG)
    kind = np.zeros((2, 2 * NH), np.float32)
    kind[0, NH:] = 1.0
    kind[1, :NH] = 1.0
    return out, kind


def sample_row_constants():
    r = np.arange(P)
    mask = (r[:, None] // DEC_S % NH == np.arange(NH)).astype(np.float32)
    sel = np.zeros((P, 2, NS), np.float32)
    for g in range(2):
        sel[r, g, g * 4 * DEC_S + r // NS * DEC_S + r % DEC_S] = 1.0
    return mask, sel


def kernel(**inputs):
    import concourse.bacc as bacc
    from concourse.bass_utils import run_bass_kernel_spmd

    x = {k: np.asarray(a) for k, a in inputs.items()}

    def columns(w, width):
        return np.ascontiguousarray(w.reshape(KD, P, -1, width).transpose(2, 1, 0, 3))

    w_in = x["w_in"][0]
    F = NH * HD
    qf, kf, vf, qd, kd, vd = (w_in[:, i * F:(i + 1) * F] for i in range(6))
    qk = np.stack([columns(a, P) for a in (qf, kf, qd, kd)]).reshape(2, 2, 4, P, KD, P)
    qk = qk.transpose(0, 2, 1, 3, 4, 5).reshape(4 * 4, P, KD, P)
    pool = x["cache_k_fox"].shape[1]
    onehot, kind = bias_row_constants()
    head_mask, row_select = sample_row_constants()
    gamma = lambda g: g.reshape(KD, P).T
    arrays = {
        "x_prompt": x["x_prompt"][0], "x_sample": x["x_sample"].reshape(NS, D),
        "w_qk": qk, "w_v": columns(np.concatenate([vf, vd], 1), 256),
        "w_f": w_in[:, 6 * F:].reshape(KD, P, NH).transpose(1, 0, 2), "b_f": x["b_fgate"].reshape(NH, 1),
        "g_attn": gamma(x["g_attn"][0]), "g_ffn": gamma(x["g_ffn"][0]),
        "g_out": gamma(np.concatenate([x["g_out_fox"][0], x["g_out_dil"][0]])),
        "g_final": x["g_final"].reshape(1, D),
        "w_out": columns(x["w_out"][0], 256), "w_query": columns(x["w_query"][0], P),
        "sub_keys": x["sub_keys"][0].transpose(2, 0, 1),
        "rel_bias": x["rel_bias"],
        "k_pages": x["cache_k_fox"][0].reshape(pool, PAGE, 4, P).transpose(0, 3, 2, 1),
        "v_pages": x["cache_v_fox"][0].reshape(pool, PAGE, F),
        "logf_pages": x["cache_logf_fox"][0].transpose(0, 2, 1),
        "k_win": x["cache_k_win"][0].reshape(DEC_B, PAST, 4, P).transpose(0, 3, 2, 1),
        "v_win": x["cache_v_win"][0].reshape(DEC_B, PAST, F),
        "page_table": x["page_table"].reshape(1, -1).astype(np.int32),
        "u_experts": x["u_experts"][0].reshape(NK, P, KD, P).transpose(0, 3, 2, 1),
        "v_experts": x["v_experts"][0].reshape(NK, P, D),
        "ident": np.eye(P, dtype=np.float32), "bucket_onehot": onehot, "row_kind": kind,
        "head_mask": head_mask, "row_select": row_select,
        "iota": np.tile(np.arange(P, dtype=np.float32), (P, 1)),
    }
    arrays = {"in_" + k: np.ascontiguousarray(a) for k, a in arrays.items()}
    outs = {"y_prompt": (SEQ, D), "y_sample": (NS, D), "lfp": (SEQ, NH), "lfs": (NS, NH)}
    for name in ("kf", "vf", "kw", "vw"):
        outs[name + "p"] = (SEQ, F)
        outs[name + "s"] = (NS, F)

    nc = bacc.Bacc("TRN2", target_bir_lowering=False, num_devices=1)
    A = {k[3:]: nc.dram_tensor(k, a.shape, mybir.dt.from_np(a.dtype), kind="ExternalInput").ap() for k, a in arrays.items()}
    O = {k: nc.dram_tensor("out_" + k, shape, F32, kind="ExternalOutput").ap() for k, shape in outs.items()}
    build(nc, A, O)
    r = run_bass_kernel_spmd(nc, [arrays], core_ids=[0]).results[0]
    got = {k: r["out_" + k] for k in outs}
    prompt = lambda a: a.reshape(1, 1, SEQ, NH, HD)
    sample = lambda a: a.reshape(1, DEC_B, DEC_S, NH, HD)
    return (got["y_prompt"].reshape(1, SEQ, D), got["y_sample"].reshape(DEC_B, DEC_S, D),
            prompt(got["kfp"]), prompt(got["vfp"]), got["lfp"].reshape(1, 1, SEQ, NH),
            sample(got["kfs"]), sample(got["vfs"]), got["lfs"].reshape(1, DEC_B, DEC_S, NH),
            prompt(got["kwp"]), prompt(got["vwp"]), sample(got["kws"]), sample(got["vws"]))
```
